# Optimizing a Trainium2 kernel written in Bass

```python
import math
import jax, jax.numpy as jnp
from jax import lax
import numpy as np

D_MODEL = 1024
BATCH = 1
SEQ = 256
DEPTH = 1

CONV_A_WIDTH = 512
CONV_A_K = 3
DN_HEADS = 8
DN_DK = 128
DN_DV = 128
DN_CONV_K = 5
CHUNK = 64
DN_QK = DN_HEADS * DN_DK
DN_VW = DN_HEADS * DN_DV
N_BRANCH = 2
D_FF = 2816
N_MOD = 9
EPS = 1e-6

SPLIT_SIZES = (
    CONV_A_WIDTH,
    CONV_A_WIDTH,
    CONV_A_WIDTH,
    2 * DN_QK + DN_VW,
    DN_VW,
    4 * DN_HEADS,
    N_BRANCH * D_MODEL,
)
IN_COLS = sum(SPLIT_SIZES)
SPLIT_OFFSETS = tuple(int(v) for v in np.cumsum(SPLIT_SIZES)[:-1])


def _rmsnorm(x, w):
    xf = x.astype(jnp.float32)
    y = xf * lax.rsqrt(jnp.mean(xf * xf, axis=-1, keepdims=True) + EPS)
    return (y * w.astype(jnp.float32)).astype(x.dtype)

def _l2norm(x):
    return x * lax.rsqrt(jnp.sum(x * x, axis=-1, keepdims=True) + EPS)

def _modulate(x, shift, scale):
    return x * (1.0 + scale) + shift

def _swiglu(x, w_up, w_down):
    a, b = jnp.split(x @ w_up, 2, axis=-1)
    return (jax.nn.silu(a) * b) @ w_down

def _dwconv(x, w):
    k_taps = w.shape[0]
    pad = k_taps // 2
    s = x.shape[1]
    xp = jnp.pad(x, ((0, 0), (pad, pad), (0, 0)))
    y = xp[:, 0:s] * w[0]
    for i in range(1, k_taps):
        y = y + xp[:, i:i + s] * w[i]
    return y

def _chunk_gated_delta(q, k, v, beta, g):
    bn, s, h, dk = q.shape
    dv = v.shape[-1]
    n = s // CHUNK

    def to_chunks(t):
        t = t.reshape((bn, n, CHUNK, h) + t.shape[3:])
        return jnp.moveaxis(t, 3, 1)

    q, k, v, beta, g = (to_chunks(t) for t in (q, k, v, beta, g))
    g = jnp.cumsum(g, axis=-1)
    idx = jnp.arange(CHUNK)
    incl = idx[:, None] >= idx[None, :]
    strict = idx[:, None] > idx[None, :]
    decay = jnp.exp(jnp.where(incl, g[..., :, None] - g[..., None, :], -jnp.inf))
    k_beta = k * beta[..., None]
    a_mat = jnp.where(strict, jnp.einsum('bhnid,bhnjd->bhnij', k_beta, k) * decay, 0.0)
    a_mat = a_mat + jnp.eye(CHUNK, dtype=q.dtype)
    rhs = jnp.concatenate([v * beta[..., None], k_beta * jnp.exp(g)[..., None]], axis=-1)
    sol = lax.linalg.triangular_solve(a_mat, rhs, left_side=True, lower=True)
    u, w = sol[..., :dv], sol[..., dv:]
    attn = jnp.einsum('bhnid,bhnjd->bhnij', q, k) * decay

    xs = tuple(jnp.moveaxis(t, 2, 0) for t in (q, k, u, w, g, attn))

    def step(state, inp):
        q_c, k_c, u_c, w_c, g_c, attn_c = inp
        v_new = u_c - jnp.einsum('bhcd,bhde->bhce', w_c, state)
        o_c = (jnp.einsum('bhcd,bhde->bhce', q_c * jnp.exp(g_c)[..., None], state)
               + jnp.einsum('bhij,bhje->bhie', attn_c, v_new))
        g_last = g_c[..., -1:]
        state = (state * jnp.exp(g_last)[..., None]
                 + jnp.einsum('bhcd,bhce->bhde', k_c * jnp.exp(g_last - g_c)[..., None], v_new))
        return state, o_c

    state0 = jnp.zeros((bn, h, dk, dv), q.dtype)
    _, o = lax.scan(step, state0, xs)
    return o.transpose(1, 0, 3, 2, 4).reshape(bn, s, h, dv)

def _hybrid_mixer(u, w_in, conv_a, conv_dn, a_log_fwd, dt_bias_fwd, a_log_bwd, dt_bias_bwd,
                  dn_norm, w_a_out, w_b_out, w_out):
    bn, s, _ = u.shape
    f32 = jnp.float32
    proj = u @ w_in
    ca_b, ca_c, ca_v, dn_qkv, dn_z, dn_ba, gate_logits = jnp.split(proj, SPLIT_OFFSETS, axis=-1)

    y_a = ca_b * _dwconv(ca_c * ca_v, conv_a)

    qkv = jax.nn.silu(_dwconv(dn_qkv, conv_dn))
    q, k, v = jnp.split(qkv, [DN_QK, 2 * DN_QK], axis=-1)
    q = (_l2norm(q.reshape(bn, s, DN_HEADS, DN_DK).astype(f32)) * (DN_DK ** -0.5))
    k = _l2norm(k.reshape(bn, s, DN_HEADS, DN_DK).astype(f32))
    v = v.reshape(bn, s, DN_HEADS, DN_DV).astype(f32)
    b_f, b_b, al_f, al_b = jnp.split(dn_ba.astype(f32), 4, axis=-1)
    beta_f, beta_b = jax.nn.sigmoid(b_f), jax.nn.sigmoid(b_b)
    g_f = -jnp.exp(a_log_fwd.astype(f32)) * jax.nn.softplus(al_f + dt_bias_fwd.astype(f32))
    g_b = -jnp.exp(a_log_bwd.astype(f32)) * jax.nn.softplus(al_b + dt_bias_bwd.astype(f32))
    o_fwd = _chunk_gated_delta(q, k, v, beta_f, g_f)
    rev = lambda t: t[:, ::-1]
    o_bwd = rev(_chunk_gated_delta(rev(q), rev(k), rev(v), rev(beta_b), rev(g_b)))
    o = _rmsnorm(o_fwd + o_bwd, dn_norm) * jax.nn.silu(dn_z.reshape(bn, s, DN_HEADS, DN_DV).astype(f32))
    y_b = o.reshape(bn, s, DN_VW).astype(u.dtype)

    gate_a, gate_b = jnp.split(gate_logits, N_BRANCH, axis=-1)
    merged = jax.nn.sigmoid(gate_a) * (y_a @ w_a_out) + jax.nn.sigmoid(gate_b) * (y_b @ w_b_out)
    return merged @ w_out

def first_inputs(seed: int = 0) -> dict:
    key = jax.random.key(seed)
    ks = jax.random.split(key, 24)
    L = DEPTH
    f32 = jnp.float32

    def nrm(k, shape, fan_in):
        return jax.random.normal(k, shape, f32) * (fan_in ** -0.5)

    def gain(k, shape):
        return 1.0 + 0.02 * jax.random.normal(k, shape, f32)

    def a_log(k):
        return jnp.log(jax.random.uniform(k, (L, DN_HEADS), f32, minval=1.0, maxval=16.0))

    def dt_bias(k):
        dt = jnp.exp(jax.random.uniform(k, (L, DN_HEADS), f32,
                                        minval=math.log(1e-3), maxval=math.log(1e-1)))
        return dt + jnp.log(-jnp.expm1(-dt))

    return {
        "x": jax.random.normal(ks[0], (BATCH, SEQ, D_MODEL), f32),
        "c": jax.random.normal(ks[1], (BATCH, D_MODEL), f32),
        "w_ada": nrm(ks[2], (L, D_MODEL, N_MOD * D_MODEL), D_MODEL),
        "b_ada": 0.02 * jax.random.normal(ks[3], (L, N_MOD * D_MODEL), f32),
        "norm_ffn1": gain(ks[4], (L, D_MODEL)),
        "w_ffn1_up": nrm(ks[5], (L, D_MODEL, 2 * D_FF), D_MODEL),
        "w_ffn1_down": nrm(ks[6], (L, D_FF, D_MODEL), D_FF),
        "norm_mix": gain(ks[7], (L, D_MODEL)),
        "w_in": nrm(ks[8], (L, D_MODEL, IN_COLS), D_MODEL),
        "conv_a": nrm(ks[9], (L, CONV_A_K, CONV_A_WIDTH), CONV_A_K),
        "conv_dn": nrm(ks[10], (L, DN_CONV_K, 2 * DN_QK + DN_VW), DN_CONV_K),
        "a_log_fwd": a_log(ks[11]),
        "dt_bias_fwd": dt_bias(ks[12]),
        "a_log_bwd": a_log(ks[13]),
        "dt_bias_bwd": dt_bias(ks[14]),
        "dn_norm": gain(ks[15], (L, DN_DV)),
        "w_a_out": nrm(ks[16], (L, CONV_A_WIDTH, D_MODEL), CONV_A_WIDTH),
        "w_b_out": nrm(ks[17], (L, DN_VW, D_MODEL), DN_VW),
        "w_out": nrm(ks[18], (L, D_MODEL, D_MODEL), D_MODEL),
        "norm_ffn2": gain(ks[19], (L, D_MODEL)),
        "w_ffn2_up": nrm(ks[20], (L, D_MODEL, 2 * D_FF), D_MODEL),
        "w_ffn2_down": nrm(ks[21], (L, D_FF, D_MODEL), D_FF),
        "norm_final": gain(ks[22], (D_MODEL,)),
    }

def first_block(x, c, w_ada, b_ada, norm_ffn1, w_ffn1_up, w_ffn1_down, norm_mix, w_in, conv_a,
              conv_dn, a_log_fwd, dt_bias_fwd, a_log_bwd, dt_bias_bwd, dn_norm, w_a_out, w_b_out,
              w_out, norm_ffn2, w_ffn2_up, w_ffn2_down, norm_final):
    h = x
    c_act = jax.nn.silu(c)
    for l in range(DEPTH):
        mod = c_act @ w_ada[l] + b_ada[l]
        sh1, sc1, g1, sh2, sc2, g2, sh3, sc3, g3 = [m[:, None, :] for m in jnp.split(mod, N_MOD, axis=-1)]
        u = _modulate(_rmsnorm(h, norm_ffn1[l]), sh1, sc1)
        h = h + 0.5 * g1 * _swiglu(u, w_ffn1_up[l], w_ffn1_down[l])
        u = _modulate(_rmsnorm(h, norm_mix[l]), sh2, sc2)
        h = h + g2 * _hybrid_mixer(u, w_in[l], conv_a[l], conv_dn[l], a_log_fwd[l], dt_bias_fwd[l],
                                   a_log_bwd[l], dt_bias_bwd[l], dn_norm[l], w_a_out[l],
                                   w_b_out[l], w_out[l])
        u = _modulate(_rmsnorm(h, norm_ffn2[l]), sh3, sc3)
        h = h + 0.5 * g3 * _swiglu(u, w_ffn2_up[l], w_ffn2_down[l])
    return _rmsnorm(h, norm_final)


DEPTH_2 = 2

N_MIXERS = 2
N_ATTN_LAYERS = (DEPTH_2 + 1) // 2
N_MLSTM_LAYERS = DEPTH_2 // 2

DA_HEADS = 8
DA_HEAD_DIM = 64
DA_V_DIM = 2 * DA_HEAD_DIM
DA_PROJ = 3 * DA_HEADS * 2 * DA_HEAD_DIM
Q_BLOCK = 128

REL_BUCKETS = 32
REL_MAX_DIST = 128

ML_HEADS = 4
ML_V_DIM = D_MODEL // ML_HEADS
ML_QK_DIM = ML_V_DIM // 2
ML_CHUNK = 64
CONV_WIDTH = 4
ML_QK_WIDTH = 2 * ML_HEADS * ML_QK_DIM
ML_V_WIDTH = ML_HEADS * ML_V_DIM
ML_PROJ = ML_QK_WIDTH + 2 * ML_V_WIDTH + 2 * ML_HEADS

D_FF_2 = 4 * D_MODEL


def rmsnorm(x, g):
    xf = x.astype(jnp.float32)
    y = xf * lax.rsqrt(jnp.mean(xf * xf, axis=-1, keepdims=True) + EPS)
    return (y * g.astype(jnp.float32)).astype(x.dtype)

def t5_causal_bucket(dist):
    max_exact = REL_BUCKETS // 2
    d = jnp.maximum(dist, 1).astype(jnp.float32)
    large = max_exact + (jnp.log(d / max_exact) / math.log(REL_MAX_DIST / max_exact)
                         * (REL_BUCKETS - max_exact)).astype(jnp.int32)
    large = jnp.minimum(large, REL_BUCKETS - 1)
    return jnp.where(dist < max_exact, dist, large)

def diff_attention(h, w_in, lq1, lk1, lq2, lk2, subln_w, w_out, rel_table, lambda_init):
    B, S, _ = h.shape
    qkv = h @ w_in
    q, k, v = jnp.split(qkv, 3, axis=-1)
    q = q.reshape(B, S, DA_HEADS, 2, DA_HEAD_DIM)
    k = k.reshape(B, S, DA_HEADS, 2, DA_HEAD_DIM)
    v = v.reshape(B, S, DA_HEADS, DA_V_DIM)
    lam = (jnp.exp(jnp.sum(lq1.astype(jnp.float32) * lk1.astype(jnp.float32)))
           - jnp.exp(jnp.sum(lq2.astype(jnp.float32) * lk2.astype(jnp.float32)))
           + lambda_init)
    scale = DA_HEAD_DIM ** -0.5
    outs = []
    for blk in range(S // Q_BLOCK):
        q0 = blk * Q_BLOCK
        kend = q0 + Q_BLOCK
        qb = q[:, q0:kend]
        kb = k[:, :kend]
        vb = v[:, :kend]
        dist = (q0 + jnp.arange(Q_BLOCK))[:, None] - jnp.arange(kend)[None, :]
        bias = rel_table[t5_causal_bucket(jnp.maximum(dist, 0))]
        bias = jnp.transpose(bias, (2, 0, 1)).astype(jnp.float32)
        logits = jnp.einsum('bqhmd,bkhmd->bmhqk', qb, kb).astype(jnp.float32) * scale + bias
        logits = jnp.where(dist >= 0, logits, -jnp.inf)
        p = jax.nn.softmax(logits, axis=-1)
        attn = p[:, 0] - lam * p[:, 1]
        outs.append(jnp.einsum('bhqk,bkhd->bqhd', attn.astype(vb.dtype), vb))
    o = jnp.concatenate(outs, axis=1)
    o = rmsnorm(o, subln_w) * (1.0 - lambda_init)
    return o.reshape(B, S, DA_HEADS * DA_V_DIM) @ w_out

def causal_depthwise_conv(x, w, b):
    C = x.shape[-1]
    y = lax.conv_general_dilated(x, w[:, None, :].astype(x.dtype), window_strides=(1,),
                                 padding=[(CONV_WIDTH - 1, 0)],
                                 dimension_numbers=('NWC', 'WIO', 'NWC'),
                                 feature_group_count=C)
    return y + b.astype(x.dtype)

def mlstm_chunkwise(q, k, v, i_pre, log_f):
    B, S, H, dk = q.shape
    dv = v.shape[-1]
    L = ML_CHUNK
    NC = S // L
    f32 = jnp.float32
    q = (q.astype(f32) * dk ** -0.5).reshape(B, NC, L, H, dk).transpose(0, 3, 1, 2, 4)
    k = k.astype(f32).reshape(B, NC, L, H, dk).transpose(0, 3, 1, 2, 4)
    v = v.astype(f32).reshape(B, NC, L, H, dv).transpose(0, 3, 1, 2, 4)
    ig = i_pre.astype(f32).reshape(B, NC, L, H).transpose(0, 3, 1, 2)
    lf = log_f.astype(f32).reshape(B, NC, L, H).transpose(0, 3, 1, 2)
    b = jnp.cumsum(lf, axis=-1)
    b_last = b[..., -1]

    a = b_last[..., None] - b + ig
    m_loc = jnp.max(a, axis=-1)
    wgt = jnp.exp(a - m_loc[..., None])
    C_loc = jnp.einsum('bhcsv,bhcsk->bhcvk', wgt[..., None] * v, k)
    n_loc = jnp.einsum('bhcs,bhcsk->bhck', wgt, k)

    def step(carry, inp):
        C, n, m = carry
        bl, Cl, nl, ml = inp
        m_new = jnp.maximum(bl + m, ml)
        decay = jnp.exp(bl + m - m_new)
        gain = jnp.exp(ml - m_new)
        C_new = decay[..., None, None] * C + gain[..., None, None] * Cl
        n_new = decay[..., None] * n + gain[..., None] * nl
        return (C_new, n_new, m_new), (C, n, m)

    init = (jnp.zeros((B, H, dv, dk), f32), jnp.zeros((B, H, dk), f32), jnp.zeros((B, H), f32))
    xs = (jnp.moveaxis(b_last, 2, 0), jnp.moveaxis(C_loc, 2, 0),
          jnp.moveaxis(n_loc, 2, 0), jnp.moveaxis(m_loc, 2, 0))
    _, (C_prev, n_prev, m_prev) = lax.scan(step, init, xs)
    C_prev = jnp.moveaxis(C_prev, 0, 2)
    n_prev = jnp.moveaxis(n_prev, 0, 2)
    m_prev = jnp.moveaxis(m_prev, 0, 2)

    causal = jnp.tril(jnp.ones((L, L), dtype=bool))
    D = b[..., :, None] - b[..., None, :] + ig[..., None, :]
    D = jnp.where(causal, D, -jnp.inf)
    m_inter = b + m_prev[..., None]
    m_j = jnp.maximum(m_inter, jnp.max(D, axis=-1))
    Sc = jnp.einsum('bhcjk,bhcsk->bhcjs', q, k) * jnp.exp(D - m_j[..., None])
    inter = jnp.exp(m_inter - m_j)
    num = (jnp.einsum('bhcjs,bhcsv->bhcjv', Sc, v)
           + inter[..., None] * jnp.einsum('bhcjk,bhcvk->bhcjv', q, C_prev))
    den = jnp.sum(Sc, axis=-1) + inter * jnp.einsum('bhcjk,bhck->bhcj', q, n_prev)
    h = num / jnp.maximum(jnp.abs(den), jnp.exp(-m_j))[..., None]
    return h.transpose(0, 2, 3, 1, 4).reshape(B, S, H, dv)

def mlstm_mixer(h, w_in, b_i, b_f, conv_w, conv_b, head_norm_w, w_out):
    B, S, _ = h.shape
    proj = h @ w_in
    qk = proj[..., :ML_QK_WIDTH]
    v = proj[..., ML_QK_WIDTH:ML_QK_WIDTH + ML_V_WIDTH]
    o_pre = proj[..., ML_QK_WIDTH + ML_V_WIDTH:ML_QK_WIDTH + 2 * ML_V_WIDTH]
    gates = proj[..., ML_QK_WIDTH + 2 * ML_V_WIDTH:].astype(jnp.float32)
    qk = jax.nn.silu(causal_depthwise_conv(qk, conv_w, conv_b))
    q = qk[..., :ML_QK_WIDTH // 2].reshape(B, S, ML_HEADS, ML_QK_DIM)
    k = qk[..., ML_QK_WIDTH // 2:].reshape(B, S, ML_HEADS, ML_QK_DIM)
    v = v.reshape(B, S, ML_HEADS, ML_V_DIM)
    i_pre = gates[..., :ML_HEADS] + b_i.astype(jnp.float32)
    log_f = jax.nn.log_sigmoid(gates[..., ML_HEADS:] + b_f.astype(jnp.float32))
    ht = mlstm_chunkwise(q, k, v, i_pre, log_f)
    ht = rmsnorm(ht, head_norm_w.reshape(ML_HEADS, ML_V_DIM))
    out = jax.nn.sigmoid(o_pre.astype(jnp.float32)) * ht.reshape(B, S, ML_V_WIDTH)
    return out.astype(h.dtype) @ w_out

def sqrelu_mlp(h, w1, w2):
    return jnp.square(jax.nn.relu(h @ w1)) @ w2

def second_inputs(seed: int = 0) -> dict:
    key = jax.random.key(seed)
    ks = jax.random.split(key, 24)
    f32 = jnp.float32
    nA, nM = N_ATTN_LAYERS, N_MLSTM_LAYERS

    def nrm(k, shape, scale):
        return jax.random.normal(k, shape, f32) * scale

    def gain(k, shape):
        return 1.0 + 0.05 * jax.random.normal(k, shape, f32)

    return {
        "x": jax.random.normal(ks[0], (BATCH, SEQ, D_MODEL), f32),
        "rel_bias": nrm(ks[1], (REL_BUCKETS, DA_HEADS), 0.5),
        "attn_norm": gain(ks[2], (nA, D_MODEL)),
        "attn_w_in": nrm(ks[3], (nA, D_MODEL, DA_PROJ), D_MODEL ** -0.5),
        "attn_lambda_q1": nrm(ks[4], (nA, DA_HEAD_DIM), 0.1),
        "attn_lambda_k1": nrm(ks[5], (nA, DA_HEAD_DIM), 0.1),
        "attn_lambda_q2": nrm(ks[6], (nA, DA_HEAD_DIM), 0.1),
        "attn_lambda_k2": nrm(ks[7], (nA, DA_HEAD_DIM), 0.1),
        "attn_subln": gain(ks[8], (nA, DA_V_DIM)),
        "attn_w_out": nrm(ks[9], (nA, DA_HEADS * DA_V_DIM, D_MODEL), (DA_HEADS * DA_V_DIM) ** -0.5),
        "mlstm_norm": gain(ks[10], (nM, D_MODEL)),
        "mlstm_w_in": nrm(ks[11], (nM, D_MODEL, ML_PROJ), D_MODEL ** -0.5),
        "mlstm_b_i": nrm(ks[12], (nM, ML_HEADS), 0.1),
        "mlstm_b_f": jnp.broadcast_to(jnp.linspace(3.0, 6.0, ML_HEADS, dtype=f32), (nM, ML_HEADS))
                     + nrm(ks[13], (nM, ML_HEADS), 0.01),
        "mlstm_conv_w": nrm(ks[14], (nM, CONV_WIDTH, ML_QK_WIDTH), CONV_WIDTH ** -0.5),
        "mlstm_conv_b": nrm(ks[15], (nM, ML_QK_WIDTH), 0.02),
        "mlstm_head_norm": gain(ks[16], (nM, ML_V_WIDTH)),
        "mlstm_w_out": nrm(ks[17], (nM, ML_V_WIDTH, D_MODEL), ML_V_WIDTH ** -0.5),
        "mlp_norm": gain(ks[18], (DEPTH_2, D_MODEL)),
        "mlp_w1": nrm(ks[19], (DEPTH_2, D_MODEL, D_FF_2), D_MODEL ** -0.5),
        "mlp_w2": nrm(ks[20], (DEPTH_2, D_FF_2, D_MODEL), D_FF_2 ** -0.5),
        "final_norm": gain(ks[21], (D_MODEL,)),
    }

def second_block(x, rel_bias, attn_norm, attn_w_in, attn_lambda_q1, attn_lambda_k1,
              attn_lambda_q2, attn_lambda_k2, attn_subln, attn_w_out,
              mlstm_norm, mlstm_w_in, mlstm_b_i, mlstm_b_f, mlstm_conv_w, mlstm_conv_b,
              mlstm_head_norm, mlstm_w_out, mlp_norm, mlp_w1, mlp_w2, final_norm):
    h = x
    for layer in range(DEPTH_2):
        j = layer // N_MIXERS
        if layer % N_MIXERS == 0:
            lambda_init = 0.8 - 0.6 * math.exp(-0.3 * layer)
            mix = diff_attention(rmsnorm(h, attn_norm[j]), attn_w_in[j],
                                 attn_lambda_q1[j], attn_lambda_k1[j],
                                 attn_lambda_q2[j], attn_lambda_k2[j],
                                 attn_subln[j], attn_w_out[j], rel_bias, lambda_init)
        else:
            mix = mlstm_mixer(rmsnorm(h, mlstm_norm[j]), mlstm_w_in[j], mlstm_b_i[j],
                              mlstm_b_f[j], mlstm_conv_w[j], mlstm_conv_b[j],
                              mlstm_head_norm[j], mlstm_w_out[j])
        h = h + mix.astype(h.dtype)
        h = h + sqrelu_mlp(rmsnorm(h, mlp_norm[layer]), mlp_w1[layer], mlp_w2[layer]).astype(h.dtype)
    return rmsnorm(h, final_norm)


def setup_inputs(seed=0):
    out = dict(first_inputs(seed))
    for name, value in second_inputs(seed + 1).items():
        if name != "x":
            out[name + "_2"] = value
    return out


def reference(
    x, c, w_ada, b_ada, norm_ffn1, w_ffn1_up, w_ffn1_down, norm_mix, w_in, conv_a, conv_dn,
    a_log_fwd, dt_bias_fwd, a_log_bwd, dt_bias_bwd, dn_norm, w_a_out, w_b_out, w_out, norm_ffn2,
    w_ffn2_up, w_ffn2_down, norm_final, rel_bias_2, attn_norm_2, attn_w_in_2, attn_lambda_q1_2,
    attn_lambda_k1_2, attn_lambda_q2_2, attn_lambda_k2_2, attn_subln_2, attn_w_out_2,
    mlstm_norm_2, mlstm_w_in_2, mlstm_b_i_2, mlstm_b_f_2, mlstm_conv_w_2, mlstm_conv_b_2,
    mlstm_head_norm_2, mlstm_w_out_2, mlp_norm_2, mlp_w1_2, mlp_w2_2, final_norm_2,
):
    x = first_block(
        x, c, w_ada, b_ada, norm_ffn1, w_ffn1_up, w_ffn1_down, norm_mix, w_in, conv_a, conv_dn,
        a_log_fwd, dt_bias_fwd, a_log_bwd, dt_bias_bwd, dn_norm, w_a_out, w_b_out, w_out,
        norm_ffn2, w_ffn2_up, w_ffn2_down, norm_final,
    )
    return second_block(
        x, rel_bias_2, attn_norm_2, attn_w_in_2, attn_lambda_q1_2, attn_lambda_k1_2,
        attn_lambda_q2_2, attn_lambda_k2_2, attn_subln_2, attn_w_out_2, mlstm_norm_2,
        mlstm_w_in_2, mlstm_b_i_2, mlstm_b_f_2, mlstm_conv_w_2, mlstm_conv_b_2,
        mlstm_head_norm_2, mlstm_w_out_2, mlp_norm_2, mlp_w1_2, mlp_w2_2, final_norm_2,
    )


_drawn_inputs = setup_inputs


def setup_inputs(seed=0):
    import zlib

    import numpy as np

    out = dict(_drawn_inputs(seed))
    spreads = {}
    factors = {'norm_ffn1': 4.169,
     'dn_norm': 8.0,
     'norm_ffn2': 7.014,
     'attn_lambda_q1_2': 8.0,
     'mlstm_norm_2': 2.844,
     'mlstm_b_i_2': 64.0,
     'mlstm_conv_b_2': 33.446,
     'mlstm_head_norm_2': 3.848}
    for name, (base, spread) in spreads.items():
        noise = np.random.default_rng([zlib.crc32(name.encode()), seed]).standard_normal(out[name].shape)
        drawn = base * np.exp(spread * noise) if base else spread * noise
        out[name] = __import__('jax').numpy.asarray(drawn.astype(out[name].dtype))
    for name, factor in factors.items():
        out[name] = (out[name] * factor).astype(out[name].dtype)
    return out
```

```python
from contextlib import ExitStack, contextmanager

import concourse.bass as bass
import numpy as np
from concourse import mybir

F32 = mybir.dt.float32
F32R = mybir.dt.float32r
ALU = mybir.AluOpType
ACT = mybir.ActivationFunctionType
AX = mybir.AxisListType

P = 128
S = 256
D = 1024
KD = D // P
FF = 2816
KF = FF // P
NMOD = 9
EPS = 1e-6
HD = 8
CH = 64
HG = 4
NEG = -1e30
FF2 = 4096
KF2 = FF2 // P
LAMBDA_INIT = 0.8 - 0.6
BUCKETS, MAX_DIST = 32, 128
ML_H = 4

SLAB = 256
SLOTS = 4
HALVES = 4

NRM = dict(ffn1=0, mix=8, ffn2=16, final=24, attn=32, mlstm=40, mlp=48, final2=64)
DN_NORM, SUBLN, HEAD_NORM, CONV2, CONV2_B = 72, 73, 74, 82, 114
ROWS1 = 122
B_ADA, CONV_A = 128, 200
ROWS2 = 84
CONV_DN = 256
ROWS3 = 120


def constants():
    r = np.arange(P)
    half, loc = r // CH, r % CH
    same = (half[:, None] == half[None, :])
    fwd = same & (loc[:, None] <= loc[None, :])
    bwd = same & (loc[:, None] >= loc[None, :])
    low = (half == 0)
    m01 = np.where(low[:, None], fwd, bwd)
    m23 = np.where(low[:, None], bwd, fwd)
    i = np.arange(CH)

    def compact(m):
        return np.stack([m[t, half[t] * CH + i] for t in range(P)])
    parts = {
        "ident": np.eye(P), "ones": np.ones((P, P)), "m01": m01, "m23": m23, "block": same,
        "lowones": np.repeat(low[:, None], P, 1), "highones": np.repeat(~low[:, None], P, 1),
        "c01": compact(m01), "c23": compact(m23),
        "identc": loc[:, None] == i[None, :],
        "strict": loc[:, None] != i[None, :],
        "neg01": np.where(compact(m01), 0.0, NEG), "neg23": np.where(compact(m23), 0.0, NEG),
        "levels": np.concatenate([((loc[:, None] // (2 * s)) == (i[None, :] // (2 * s)))
                                  & ((loc[:, None] // s) != (i[None, :] // s))
                                  for s in (1, 2, 4, 8, 16, 32)], 1),
    }
    at, cols = {}, 0
    for k, v in parts.items():
        at[k] = (cols, v.shape[1])
        cols += v.shape[1]
    return np.concatenate([np.asarray(v, np.float32) for v in parts.values()], 1), at


def constants2():
    q = np.arange(P)
    y = np.arange(384)
    dist = 255 - y
    exact = BUCKETS // 2
    d = np.maximum(dist, 1).astype(np.float32)
    large = exact + (np.log(d / exact) / np.float32(np.log(MAX_DIST / exact)) * (BUCKETS - exact)).astype(np.int32)
    bucket = np.where(dist < exact, dist, np.minimum(large, BUCKETS - 1))
    onehot = np.zeros((P, 384), np.float32)
    for b in range(BUCKETS):
        onehot[b] = (bucket == b) & (dist >= 0)
    k = np.arange(S)
    causal = np.where(P - k[None, :] + q[:, None] >= 0, 0.0, NEG)
    after = np.where(k[None, :] >= q[:, None], 0.0, NEG)
    sel = np.zeros((P, ML_H, P), np.float32)
    for h in range(ML_H):
        sel[h, h, :] = 1.0
    parts = {"onehot": onehot, "causal": causal, "after": after, "sel": sel.reshape(P, -1)}
    at, cols = {}, 0
    for n, v in parts.items():
        at[n] = (cols, v.shape[1])
        cols += v.shape[1]
    return np.concatenate([np.asarray(v, np.float32) for v in parts.values()], 1), at


class Chain:

    def __init__(self, engine, sem):
        self.engine, self.sem, self.n, self.i, self.per = engine, sem, 0, 0, 0

    def link(self, instruction):
        instruction.then_inc(self.sem, 1)
        self.n += 1
        self.engine.wait_ge(self.sem, self.n + self.i * self.per)


class Follow:

    def __init__(self, engine, sem):
        self.engine, self.sem, self.n, self.i, self.per = engine, sem, {}, 0, {}

    def next(self, name):
        self.n[name] = self.n.get(name, 0) + 1
        self.engine.wait_ge(self.sem(name), self.n[name] + self.i * self.per.get(name, 0))

    @contextmanager
    def loop(self, iters, chain=None, links=0, **per):
        start, first = dict(self.n), chain.n if chain else 0
        with self.engine.Fori(0, iters) as i:
            self.i, self.per = i, per
            if chain:
                chain.i, chain.per = i, links
            yield i
        for k in per:
            assert self.n[k] - start.get(k, 0) == per[k], (k, self.n[k] - start.get(k, 0))
            self.n[k] = start.get(k, 0) + per[k] * iters
        if chain:
            assert chain.n - first == links, (chain.n - first, links)
            chain.n, chain.i, chain.per = first + links * iters, 0, 0
        self.i, self.per = 0, {}


class Cursor:

    def __init__(self, engine, chain=None):
        self.e, self.chain = engine, chain
        self.slot_uses, self.half, self.bank_uses, self.i = [0] * SLOTS, 0, [1, 1], 0

    @contextmanager
    def repeat(self, iters, slots, splits, banks, links=0):
        self.slots, self.splits, self.banks = slots, splits, banks
        self.step = [slots.count(r) for r in range(SLOTS)]
        self.bank_step = [banks.count(b) for b in range(2)]
        start = self.chain.n if self.chain else 0
        if iters > 1:
            if self.chain:
                self.chain.per = links
            with self.e.Fori(0, iters) as i:
                self.i = i
                if self.chain:
                    self.chain.i = i
                yield i
            if self.chain:
                assert self.chain.n - start == links, (self.chain.n - start, links)
                self.chain.n = start + links * iters
                self.chain.i, self.chain.per = 0, 0
        else:
            yield 0
        self.i = 0
        self.slot_uses = [u + n * iters for u, n in zip(self.slot_uses, self.step)]
        self.bank_uses = [u + n * iters for u, n in zip(self.bank_uses, self.bank_step)]
        self.half += 2 * len(splits) * iters

    def skip(self, iters, slots, splits, banks):
        self.slot_uses = [u + slots.count(r) * iters for r, u in enumerate(self.slot_uses)]
        self.bank_uses = [u + banks.count(b) * iters for b, u in enumerate(self.bank_uses)]
        self.half += 2 * len(splits) * iters

    def use(self, j):
        r = self.slots[j]
        return r, self.i * self.step[r] + (self.slot_uses[r] + self.slots[:j].count(r))

    def split_no(self, n):
        return self.i * len(self.splits) + (self.half // 2 + n)

    def half_of(self, n):
        return self.i * (2 * len(self.splits)) + (self.half + 2 * n)

    def next_split(self, n):
        if n + 1 < len(self.splits):
            r, k = self.use(self.splits[n + 1])
        else:
            r = self.slots[self.splits[0]]
            k = self.i * self.step[r] + (self.slot_uses[r] + self.step[r])
        return r, k, self.half_of(n + 1)

    def bank_use(self, g):
        b = self.banks[g]
        return b, self.i * self.bank_step[b] + (self.bank_uses[b] + self.banks[:g].count(b))


def build(nc, A, out):
    ctx = ExitStack()
    KB = 1024
    reserved = 16 * KB
    end = 224 * KB - reserved

    def at(name, shape, dt, offset):
        size = 4 * int(np.prod(shape[1:]))
        assert offset + size <= end, (name, offset, size)
        return nc.alloc_sbuf_tensor_at(name, shape, dt, offset=reserved + offset).ap()

    with ctx:
        ctx.enter_context(nc.allow_non_contiguous_dma("parameter rows"))
        raw = [at(f"raw{i}", [P, 8, SLAB], F32, 8 * KB * i) for i in range(SLOTS)]
        w_hi = [at(f"w_hi{i}", [P, 4, SLAB], F32R, (32 + 4 * i) * KB) for i in range(HALVES)]
        w_lo = [at(f"w_lo{i}", [P, 4, SLAB], F32R, (48 + 4 * i) * KB) for i in range(HALVES)]
        hT = at("hT", [P, KD, S], F32, 64 * KB)
        u_hi = at("u_hi", [P, KD, S], F32R, 72 * KB)
        u_lo = at("u_lo", [P, KD, S], F32R, 80 * KB)
        uf = at("uf", [P, KD, S], F32, 88 * KB)
        x_tm = at("x_tm", [P, 2, D], F32, 88 * KB)
        C_np, C_at = constants()
        cst = at("cst", [P, C_np.shape[1]], F32, 96 * KB)
        o = 96 * KB + 4 * C_np.shape[1]
        small = {}

        def sm(name, shape, dt=F32):
            nonlocal o
            small[name] = at(name, shape, dt, o)
            o += (4 * int(np.prod(shape[1:])) + 31) // 32 * 32
            return small[name]
        prm = sm("prm", [P, 3 * P])
        modc = sm("modc", [P, NMOD * KD])
        cact = sm("cact", [P, KD])
        gcol = sm("gcol", [P, 4 * KD])
        cc = sm("cc", [P, 4])
        abc = sm("abc", [P, 4, HD])
        rms = sm("rms", [P, S])
        rstd = sm("rstd", [P, S])
        sil = sm("sil", [P, 2, S])
        mt = sm("mt", [P, 2, S])

        relt = sm("relt", [P, 8])
        lamv = sm("lamv", [P, 4, 64])
        lam = sm("lam", [P, 8])
        stat = sm("stat", [P, 40])
        bif = sm("bif", [4, 2])
        wg2 = sm("wg2", [P, KD, 2 * ML_H])
        wba = sm("wba", [P, KD, 4 * HD])
        act_mark = sm("act_mark", [P, 1])
        marks = sm("marks", [P, 2 * SLOTS])
        big = (o + 31) // 32 * 32

        def cs(name):
            a, n = C_at[name]
            return cst[:, a:a + n]

        mid_hi = at("mid_hi", [P, KF2, S], F32R, big)
        mid_lo = at("mid_lo", [P, KF2, S], F32R, big + 32 * KB)
        mt2 = at("mt2", [P, 2, S], F32, big + 84 * KB)
        sil2 = at("sil2", [P, 2, S], F32, big + 86 * KB)
        prow = at("prow", [P, 3, P], F32, big)
        acc = at("acc", [P, 28 * SLAB], F32, big + 54 * KB)
        qkv = at("qkv", [P, 3 * HD, S], F32, big)
        zs = at("zs", [P, HD, S], F32, big + 24 * KB)
        gt = at("gt", [P, 2 * KD, S], F32, big + 32 * KB)
        ca = at("ca", [P, 12, S], F32, big + 48 * KB)
        pad = [at(f"pad{i}", [P, 2, S + 4], F32, big + 60 * KB + 2112 * i) for i in range(2)]
        cacc = [at(f"cacc{i}", [P, 2, S], F32, big + 64 * KB + 256 + 2048 * i) for i in range(2)]
        acc8 = at("acc8", [P, 8 * SLAB], F32, big + 68 * KB + 256)
        cv = at("cv", [P, 4, S + 2], F32, big + 76 * KB + 256)
        tok = at("tok", [P, 12, 32], F32, big + 82 * KB)
        yaf = at("yaf", [P, 4, S], F32, big + 84 * KB)
        ya_hi = at("ya_hi", [P, 4, S], F32R, big + 88 * KB)
        ya_lo = at("ya_lo", [P, 4, S], F32R, big + 60 * KB)
        ktm = at("ktm", [P, 2, HG, P], F32, big + 48 * KB)
        vtm = at("vtm", [P, 2, HG, P], F32, big + 52 * KB)
        kk = at("kk", [P, 2, 2, HG, CH], F32, big + 56 * KB)
        dec = at("dec", [P, 4, HG, CH], F32, big + 60 * KB)
        r_exp = at("r_exp", [P, 4, HG, P], F32, big + 56 * KB)
        bmat = at("bmat", [P, 4, HG, CH], F32, big + 64 * KB)
        tmpc = at("tmpc", [P, 4, HG, CH], F32, big + 68 * KB)
        a_exp = at("a_exp", [P, 4, HG, P], F32, 72 * KB)
        t_exp = at("t_exp", [P, 4, HG, P], F32, 80 * KB)
        att_exp = at("att_exp", [P, 4, HG, P], F32, 88 * KB)
        pcs = at("pcs", [P, 4, HG, CH], F32, big + 72 * KB)
        qtm = at("qtm", [P, 2, HG, P], F32, big + 72 * KB)
        osq = at("osq", [P, 2, HG, P], F32, 72 * KB)
        st = at("st", [P, 2, HG, P], F32, big + 64 * KB)
        oacc = at("oacc", [P, 2, HG, P], F32, big + 68 * KB)
        rr = at("rr", [P, HG, P], F32, big + 72 * KB)
        vn = at("vn", [P, HG, P], F32, big + 74 * KB)
        t1 = at("t1", [P, HG, P], F32, big + 79 * KB)
        vns = at("vns", [P, HG, P], F32, 80 * KB)
        t2 = at("t2", [P, HG, P], F32, 82 * KB)
        t3 = at("t3", [P, HG, P], F32, 84 * KB)
        mg_hi = at("mg_hi", [P, KD, S], F32R, big + 8 * KB)
        mg_lo = at("mg_lo", [P, KD, S], F32R, big + 16 * KB)

        qa = at("qa", [P, 24, S], F32, big)
        vt2 = at("vt2", [P, 2, 8, P], F32, big + 24 * KB)
        tz = at("tz", [P, 8, 384], F32, big + 32 * KB)
        sc2 = [at(f"sc2_{i}", [P, 2, 384], F32, big + (44 + 3 * i) * KB) for i in range(2)]
        aa = [at(f"aa{i}", [P, 384], F32, big + 50 * KB + 1536 * i) for i in range(2)]
        a1t = at("a1t", [P, 384], F32, big + 53 * KB)
        aT = at("aT", [P, 384], F32, big + 55 * KB)
        otm = at("otm", [P, 2, 8, P], F32, big + 57 * KB)
        osq2 = at("osq2", [P, 2, 8, P], F32, big + 44 * KB)
        C2_np, C2_at = constants2()
        cst2 = at("cst2", [P, C2_np.shape[1] - 384], F32, big + 66 * KB)
        onehot = at("onehot", [P, 384], F32, big + 8 * KB)
        brow = at("brow", [8, 384], F32, big + 10 * KB)
        bias_dram = nc.dram_tensor("bias_rows", (8, P, 384), F32, kind="Internal").ap()
        qk2 = at("qk2", [P, 8, S], F32, big)
        vo = at("vo", [P, 16, S], F32, big + 8 * KB)
        vt3 = at("vt3", [P, 2, 8, P], F32, big + 24 * KB)
        pad2 = [at(f"pad2_{i}", [P, 2, S + 4], F32, big + 32 * KB + 2112 * i) for i in range(2)]
        cac2 = [at(f"cac2_{i}", [P, 2, S], F32, big + 37 * KB + 2048 * i) for i in range(2)]
        rows2 = at("rows2", [4, 9, S], F32, big + 41 * KB)
        acol = at("acol", [P, 2, ML_H], F32, big + 50 * KB)
        ex2 = at("ex2", [P, 384], F32, big + 51 * KB)
        sct = at("sct", [P, 384], F32, big + 53 * KB)
        nsq = at("nsq", [P, 2, S], F32, big + 55 * KB)
        dn = at("dn", [P, S], F32, big + 57 * KB)
        d2 = at("d2", [P, S], F32, big + 58 * KB)
        rt = at("rt", [P, S], F32, big + 59 * KB)
        yh = at("yh", [P, 2, S], F32, big + 60 * KB)

        def cs2(name):
            a, n = C2_at[name]
            return cst2[:, a - 384:a - 384 + n]

        ps = [ctx.enter_context(nc.psum_tensor(f"ps{i}", [P, 512], F32)) for i in range(8)]

        def bank(i):
            return ps[i][:, :]

        SEM = {}

        def s(name):
            if name not in SEM:
                SEM[name] = ctx.enter_context(nc.semaphore(name))
            return SEM[name]

        raw_loaded = [s(f"raw_loaded{r}") for r in range(SLOTS)]
        slab_taken = [s(f"slab_taken{r}") for r in range(SLOTS)]
        bank_free = [s(f"bank_free{b}") for b in range(2)]
        halves_free = s("halves_free")
        hi_ready = s("hi_ready")
        lo_ready = [s("lo_ready0"), s("lo_ready1")]
        NPAR = 16
        block = ctx.enter_context(nc.Block())

        w_ada, w_in = A["w_ada"][0], A["w_in"][0]
        HEAD_DVE, HEAD_POOL = (0, 2), (1, 3)
        DOWN_ADA = [0, 1, 2, 3, 3, 0, 1, 2, 3, 3]
        DOWN_SPLIT = [0, 1, 2, 5, 6, 7]

        def kpn(w):
            return w.rearrange("(k p) n -> p k n", p=P)

        def tail(sp):
            sp.wait_ge(s("y_ready"), 1)
            sp.dma_start(out[0].rearrange("(t p) d -> p t d", p=P), x_tm).then_inc(s("stored"), 16)
            sp.wait_ge(s("stored"), 16)

        WBA = A["w_in"][0].rearrange("(k p) n -> p k n", p=P)[:, :, 5632:5664]
        SIX = [0, 1, 2, 0, 1, 2]
        ZG = [0, 1, 3, 2, 3, 0, 3, 1, 3, 2]
        ZG_SPLIT = [0, 1, 3, 5, 7, 9]
        TB, TX, TAB, TE, TG, TGN, TBN, TGS, TEG, TED, TES = range(11)

        def tk(r, n=32):
            return tok[:, r, 0:n]

        def pair(ap, p):
            return ap.rearrange("q (c t) -> q c t", c=4)[:, p:4 - p:3 - 2 * p, :]

        def pslice(ap, p):
            return ap[:, p * P:(p + 1) * P]

        def chunk(ap, c):
            o = (0, 2, 3, 1)[c] * CH
            return ap[:, o:o + CH]

        PAIR = [0, 1, 1, 0]
        SIDES = (slice(0, CH), slice(CH, P))

        def side_of(n, d):
            return d if n < 2 else 1 - d

        @block.sync
        def _(sp):
            cur = Cursor(sp)
            sp.dma_start(cst, A["consts"]).then_inc(s("consts_in"), 16)
            sp.dma_start(wba, WBA).then_inc(s("wba_in"), 16)

            def load(j, w, k0, nk, col):
                r, k = cur.use(j)
                if not isinstance(col, int):
                    col = sp.snap(col)
                sp.wait_ge(slab_taken[r], k * 2 + 2)
                sp.dma_start(raw[r][:, 0:nk, :], kpn(w)[:, k0:k0 + nk, bass.ds(col, SLAB)])\
                    .then_inc(raw_loaded[r], 16)

            with cur.repeat(2, [0, 1, 2, 3], [], []) as i:
                for j in range(4):
                    load(j, w_ada, 0, 8, i * 1024 + j * SLAB)

            def ffn_up(w, ada):
                if ada:
                    with cur.repeat(11, [0, 1, 2], [0, 1], [0, 1]) as i:
                        load(0, w, 0, 8, i * SLAB)
                        load(1, w, 0, 8, i * SLAB + FF)
                        load(2, w_ada, 0, 8, i * SLAB + 8 * SLAB)
                else:
                    with cur.repeat(11, [0, 1], [0, 1], [0, 1]) as i:
                        load(0, w, 0, 8, i * SLAB)
                        load(1, w, 0, 8, i * SLAB + FF)

            def k_groups(w, iters, kt, slots, banks, ada=False):
                n = (kt + 7) // 8
                splits = DOWN_SPLIT if ada else list(range(2 * n))
                with cur.repeat(iters, slots, splits, banks) as i:
                    for j in range(len(slots)):
                        if j in splits:
                            g, q = divmod(splits.index(j), n)
                            load(j, w, 8 * q, min(8, kt - 8 * q), i * (2 * SLAB) + g * SLAB)
                        else:
                            g, q = divmod(j, len(slots) // 2)
                            load(j, w_ada, 0, 8, i * (4 * SLAB) + (20 + 2 * g + q - 3) * SLAB)

            ffn_up(A["w_ffn1_up"][0], True)
            with cur.repeat(1, [3], [], []):
                load(0, w_ada, 0, 8, 19 * SLAB)
            k_groups(A["w_ffn1_down"][0], 2, KF, DOWN_ADA, [0, 1], True)
            with cur.repeat(1, SIX, range(6), [0, 1] * 3):
                for j in range(6):
                    load(j, w_in, 0, 8, j * SLAB)
            with cur.repeat(2, SIX, range(6), [0, 1] * 3) as i:
                for j in range(6):
                    load(j, w_in, 0, 8, i * 1536 + (1536 + j * SLAB))
            with cur.repeat(2, ZG, ZG_SPLIT, [0, 1] * 3) as i:
                for j in range(10):
                    n = ZG_SPLIT.index(j) if j in ZG_SPLIT else None
                    if n is None:
                        load(j, w_ada, 0, 8, i * (4 * SLAB) + (28 + j // 2 - 1) * SLAB)
                    elif n < 2:
                        load(j, w_in, 0, 8, i * 512 + (4608 + n * SLAB))
                    else:
                        load(j, w_in, 0, 8, i * 1024 + (5664 + (n - 2) * SLAB))
            with cur.repeat(1, [0, 1], [0, 1], [0, 1, 0, 1]):
                for j in range(2):
                    r, k = cur.use(j)
                    sp.wait_ge(slab_taken[r], k * 2 + 2)
                    for h, signal in enumerate((s("wa_first"), raw_loaded[r])):
                        c = (2 * j + h) * SLAB
                        sp.dma_start(raw[r][:, 4 * h:4 * h + 4, :], kpn(A["w_a_out"][0])[:, :, c:c + SLAB])\
                            .then_inc(signal, 16)
                        if h == 0:
                            sp.wait_ge(s("wa_first"), 16 * (j + 1))
            for w in ("w_b_out", "w_out"):
                with cur.repeat(1, [0, 1, 2, 3], range(4), [0, 1] * 2):
                    for j in range(4):
                        load(j, A[w][0], 0, 8, j * SLAB)
            ffn_up(A["w_ffn2_up"][0], False)
            k_groups(A["w_ffn2_down"][0], 2, KF, SIX, [0, 1])
            sp.dma_start(cst2, A["consts2"][:, 384:]).then_inc(s("consts2_in"), 16)

            def columns(w, iters, n, col=0):
                slots = SIX if n == 6 else list(range(4))
                with cur.repeat(iters, slots, range(n), [0, 1] * (n // 2)) as i:
                    for j in range(n):
                        load(j, w, 0, 8, i * (n * SLAB) + (col + j * SLAB))

            def mlp(layer):
                columns(A["mlp_w1_2"][layer], 4, 4)
                if layer == 0:
                    k_groups(A["mlp_w2_2"][layer], 2, KF2, [0, 1, 2, 3] * 2, [0, 1])
                else:
                    for half in range(2):
                        with cur.repeat(1, [0, 1, 2, 3] * 2, range(8), [0, 1]):
                            for j in range(8):
                                load(j, A["mlp_w2_2"][layer], 8 * (j % 4), 8, (2 * half + j // 4) * SLAB)
            columns(A["attn_w_in_2"][0], 2, 6)
            columns(A["attn_w_out_2"][0], 1, 4)
            mlp(0)
            columns(A["mlstm_w_in_2"][0], 1, 4)
            columns(A["mlstm_w_in_2"][0], 2, 4, 4 * SLAB)
            columns(A["mlstm_w_out_2"][0], 1, 4)
            mlp(1)
            tail(sp)

        def arrived(e, r, k):
            e.wait_ge(raw_loaded[r], k * 16 + 16)

        @block.gpsimd
        def _(pool):
            cur = Cursor(pool)

            def split_lo(r, k, u):
                pool.wait_ge(hi_ready, u + 2)
                half = (cur.stat + 1) % HALVES
                pool.tensor_tensor(w_lo[half], raw[r][:, 4:8, :], w_hi[half].bitcast(F32),
                                   ALU.subtract).then_inc(lo_ready[1], 1)
                pool.memset(marks[:, SLOTS + r:SLOTS + r + 1], 0.0).then_inc(slab_taken[r], 1)

            def walk(iters, slots, splits, banks, last=False):
                with cur.repeat(iters, slots, splits, banks):
                    for n in range(len(splits) - last):
                        r, k, u = cur.next_split(n)
                        cur.stat = cur.half + 2 * (n + 1)
                        split_lo(r, k, u)

            four, eight = [0, 1, 2, 3], [0, 1, 2, 3] * 2
            chain = Chain(pool, s("pool_order"))
            head = Cursor(pool, chain)
            with head.repeat(2, four, [], [], 2 * len(HEAD_POOL)) as i:
                for m, j in enumerate(HEAD_POOL):
                    x = raw[j]
                    pool.wait_ge(s("ada_scaled"), i * len(HEAD_POOL) + (m + 1))
                    for n in (4, 2):
                        pool.nop(nofuse=True)
                        chain.link(pool.tensor_tensor(x[:, 0:n, :], x[:, 0:n, :], x[:, n:2 * n, :], ALU.add))
                    pool.nop(nofuse=True)
                    pool.tensor_tensor(acc[:, bass.ds(i * 1024 + j * SLAB, SLAB)], x[:, 0, :], x[:, 1, :], ALU.add)\
                        .then_inc(slab_taken[j], 2)
            pool.memset(marks[:, 0:1], 0.0).then_inc(s("ada_done"), 2 * len(HEAD_POOL))
            cur.skip(2, four, [], [])
            cur.stat = 0
            split_lo(0, cur.slot_uses[0], 0)
            walk(11, [0, 1, 2], [0, 1], [0, 1])
            cur.skip(1, [3], [], [])
            walk(2, DOWN_ADA, DOWN_SPLIT, [0, 1])
            walk(1, SIX, range(6), [0, 1] * 3)
            walk(2, SIX, range(6), [0, 1] * 3)
            walk(2, ZG, ZG_SPLIT, [0, 1] * 3)
            walk(1, [0, 1], [0, 1], [0, 1, 0, 1])
            walk(1, four, range(4), [0, 1] * 2)
            walk(1, four, range(4), [0, 1] * 2)
            walk(11, [0, 1], [0, 1], [0, 1])
            walk(2, SIX, range(6), [0, 1])
            walk(2, SIX, range(6), [0, 1] * 3)
            walk(1, four, range(4), [0, 1] * 2)
            walk(4, four, range(4), [0, 1] * 2)
            walk(2, eight, range(8), [0, 1])
            walk(1, four, range(4), [0, 1] * 2)
            walk(2, four, range(4), [0, 1] * 2)
            walk(1, four, range(4), [0, 1] * 2)
            walk(4, four, range(4), [0, 1] * 2)
            walk(1, eight, range(8), [0, 1])
            walk(1, eight, range(8), [0, 1], last=True)

        @block.tensor
        def _(pe):
            cur = Cursor(pe)
            pe.wait_ge(s("consts_in"), 16)
            pe.wait_ge(s("params_in"), 16 * NPAR)
            for j, rows in enumerate((ROWS1, ROWS2, ROWS3)):
                mm = pe.transpose(bank(2)[:, j * P:j * P + rows], prow[0:rows, j, :], cs("ident")[0:rows, 0:rows])
            mm.then_inc(s("prm_T"), 1)
            pe.wait_ge(s("bias_in"), 32)
            pe.matmul(bank(7)[0:8, 0:384], relt[0:BUCKETS, :], onehot[0:BUCKETS, :], start=True, stop=True)\
                .then_inc(s("brow_ps"), 1)
            pe.wait_ge(s("x_in"), 16)
            for k in range(KD):
                for t in range(2):
                    mm = pe.transpose(bank(3 + k // 2)[:, (k % 2) * S + t * P:(k % 2) * S + (t + 1) * P],
                                      x_tm[:, t, k * P:(k + 1) * P], cs("ident"))
                    if k == 0 and t == 0:
                        mm.then_inc(halves_free, HALVES)
            mm.then_inc(s("x_T"), 1)
            pe.wait_ge(s("c_ready"), 1)

            def mod_sums(first, n, bnk, done):
                pe.wait_ge(s("ada_done"), done)
                pe.wait_ge(s("h_ready"), 1)
                for c in range(2 * n):
                    mm = pe.matmul(bank(bnk)[:, c:c + 1], acc[:, (first * 2 + c) * P:(first * 2 + c + 1) * P],
                                   cs("ones")[:, 0:1], start=True, stop=True)
                mm.then_inc(s("mod_ps"), 1)

            def slab(j, n, g, k0, nk, first, last, hi, lo, ready=None):
                r, k = cur.use(j)
                b, uses = cur.bank_use(g)
                if first:
                    pe.wait_ge(bank_free[b], uses)
                for h in range(2):
                    ks = range(4 * h, min(4 * h + 4, nk))
                    pe.wait_ge(lo_ready[h], cur.split_no(n) + 1)
                    half = (cur.half + 2 * n + h) % HALVES
                    for m in range(2):
                        for kt in ks:
                            if m == 0 and ready and kt % 2 == 0:
                                pe.wait_ge(ready[0], ready[1] + (k0 + kt) // 2 + 1)
                            cols = slice(m * P, (m + 1) * P)
                            a, b_ = w_hi[half][:, kt % 4, cols], w_lo[half][:, kt % 4, cols]
                            for q, (x, y) in enumerate(((a, hi), (a, lo), (b_, hi))):
                                mm = pe.matmul(bank(b)[:, m * S:(m + 1) * S], x, y[:, k0 + kt, :],
                                               start=(first and h == 0 and m == 0 and kt == 0 and q == 0),
                                               stop=(last and kt == nk - 1 and q == 2),
                                               skip_group_check=True)
                    mm.then_inc(halves_free, 1)

            cur.skip(2, [0, 1, 2, 3], [], [])
            mod_sums(0, 8, 7, 8)

            norm_n = [0, 0]

            def warm(n):
                for _ in range(n):
                    pe.matmul(bank(0), cs("ident"), cst[:, 0:512], start=True, stop=True, skip_group_check=True)

            def bank_0_read():
                pe.wait_ge(bank_free[0], cur.bank_uses[0])

            def norm(split=True, meanwhile=None):
                n = norm_n[0] = norm_n[0] + 1
                norm_n[1] += split
                bank_0_read()
                warm(2)
                for k in range(KD):
                    if k % 4 == 0:
                        pe.wait_ge(s("sq_ready"), 2 * (n - 1) + k // 4 + 1)
                    mm = pe.matmul(bank(2)[:, 0:S], cs("ones"), uf[:, k, :], start=(k == 0), stop=(k == KD - 1))
                mm.then_inc(s("ss_ready"), 1)
                if meanwhile:
                    meanwhile()
                elif split:
                    warm(10)

            def ffn(with_ada, mids):
                norm()
                ready = (s("u_ready"), 4 * (norm_n[1] - 1))
                with cur.repeat(11, [0, 1, 2] if with_ada else [0, 1], [0, 1], [0, 1]) as i:
                    slab(0, 0, 0, 0, 8, True, True, u_hi, u_lo, ready)
                    slab(1, 1, 1, 0, 8, True, True, u_hi, u_lo)
                if with_ada:
                    cur.skip(1, [3], [], [])
                    mod_sums(8, 4, 7, 19)
                mids = (s("mid_ready"), mids)
                slots = DOWN_ADA if with_ada else [0, 1, 2] * 2
                splits = DOWN_SPLIT if with_ada else list(range(6))
                with cur.repeat(2, slots, splits, [0, 1]) as i:
                    for g in range(2):
                        for q in range(3):
                            slab(splits[3 * g + q], 3 * g + q, g, 8 * q, min(8, KF - 8 * q), q == 0, q == 2, mid_hi, mid_lo,
                                 mids)

            follow = Follow(pe, s)

            def mixer_mods():
                mod_sums(12, 8, 7, 28)
                mod_sums(20, 8, 6, 28)

            def mixer():
                ready = (s("u_ready"), 4 * (norm_n[1] - 1))
                pe.wait_ge(s("wba_in"), 16)
                pe.wait_ge(ready[0], ready[1] + 4)
                for p in range(2):
                    for side, rows in enumerate(SIDES):
                        c = 3 - p if side else p
                        for kt in range(KD):
                            mm = pe.matmul(bank(3)[rows, 32 * p:32 * p + 32], uf[:, kt, c * CH:(c + 1) * CH],
                                           wba[:, kt, :], start=(kt == 0), stop=(kt == KD - 1))
                mm.then_inc(s("ba_ps"), 1)
                with cur.repeat(1, SIX, range(6), [0, 1] * 3):
                    for j in range(6):
                        slab(j, j, j, 0, 8, True, True, u_hi, u_lo)
                pe.wait_ge(s("g_ready"), 1)
                pe.matmul(bank(4)[:, 0:16], cs("m01"), tk(TGN)[:, 0:16], start=True, stop=True)
                pe.matmul(bank(4)[:, 16:32], cs("m23"), tk(TGN)[:, 16:32], start=True, stop=True)
                for c, m in enumerate(("block", "lowones", "highones")):
                    mm = pe.matmul(bank(4)[:, 32 + 32 * c:64 + 32 * c], cs(m), tk(TGN), start=True, stop=True)
                mm.then_inc(s("g_ps"), 1)
                with cur.repeat(2, SIX, range(6), [0, 1] * 3):
                    for j in range(6):
                        slab(j, j, j, 0, 8, True, True, u_hi, u_lo)
                with cur.repeat(2, ZG, ZG_SPLIT, [0, 1] * 3):
                    for n, j in enumerate(ZG_SPLIT):
                        slab(j, n, n, 0, 8, True, True, u_hi, u_lo)
                pe.wait_ge(s("ada_done"), 36)
                for c in range(16):
                    mm = pe.matmul(bank(7)[:, c:c + 1], acc8[:, c * P:(c + 1) * P], cs("ones")[:, 0:1],
                                   start=True, stop=True)
                mm.then_inc(s("mod_ps"), 1)
                pe.wait_ge(s("ya_ready"), 1)
                with cur.repeat(1, [0, 1], [0, 1], [0, 1, 0, 1]):
                    for j in range(2):
                        r, k = cur.use(j)
                        for h in range(2):
                            b, uses = cur.bank_use(2 * j + h)
                            pe.wait_ge(bank_free[b], uses)
                            pe.wait_ge(lo_ready[h], cur.split_no(j) + 1)
                            half = (cur.half + 2 * j + h) % HALVES
                            for m in range(2):
                                for kt in range(4):
                                    cols = slice(m * P, (m + 1) * P)
                                    x, y = w_hi[half][:, kt, cols], w_lo[half][:, kt, cols]
                                    for q, (a, v) in enumerate(((x, ya_hi), (x, ya_lo), (y, ya_hi))):
                                        mm = pe.matmul(bank(b)[:, m * S:(m + 1) * S], a, v[:, kt, :],
                                                       start=(m == 0 and kt == 0 and q == 0),
                                                       stop=(kt == 3 and q == 2), skip_group_check=True)
                            mm.then_inc(halves_free, 1)
                bank_0_read()
                for hh in range(HD // HG):
                    delta(hh)
                follow.next("d_dp")
                with cur.repeat(1, [0, 1, 2, 3], range(4), [0, 1] * 2):
                    pe.wait_ge(s("yb_ready"), 2)
                    for j in range(4):
                        slab(j, j, j, 0, 8, True, True, u_hi, u_lo)
                with cur.repeat(1, [0, 1, 2, 3], range(4), [0, 1] * 2):
                    for j in range(4):
                        slab(j, j, j, 0, 8, True, True, mg_hi, mg_lo, (s("mg_ready"), 0) if j == 0 else None)

            def delta(hh):
                H = [hh * HG + h for h in range(HG)]
                idn = cs("ident")
                if hh:
                    follow.next("d_dp")
                else:
                    pe.wait_ge(s("silu_done"), 2 + 12)
                for t, base in enumerate((HD, 0, 2 * HD)):
                    for p in range(2):
                        for h in range(HG):
                            mm = pe.transpose(bank(2 + 2 * t + p)[:, h * P:(h + 1) * P],
                                              pslice(qkv[:, base + H[h], :], p), idn)
                        mm.then_inc(s("d_pa"), 1)
                for t, x in enumerate((ktm, qtm)):
                    for p in range(2):
                        follow.next("d_dp")
                        for h in range(HG):
                            mm = pe.transpose(bank(2 + 2 * t + p)[:, h * P:(h + 1) * P], x[:, p, h, :], idn)
                        mm.then_inc(s("d_pa"), 1)
                for _ in range(4):
                    follow.next("d_ap")
                for p in range(2):
                    for h in range(HG):
                        for side in range(2):
                            c = 3 - p if side else p
                            kc = chunk(qkv[:, HD + H[h], :], c)
                            o = (p * HG + h) * CH
                            pe.matmul(bank(6)[SIDES[side], o:o + CH], kc, kc, start=True, stop=True)
                            mm = pe.matmul(bank(7)[SIDES[side], o:o + CH], kc, chunk(qkv[:, H[h], :], c),
                                           start=True, stop=True)
                mm.then_inc(s("d_pa"), 1)
                for b in (2, 4):
                    follow.next("d_dp")
                    for j in range(2):
                        mm = pe.matmul(bank(b + j), cs("block"), tmpc[:, 2 * j:2 * j + 2].rearrange("q n h c -> q (n h c)"),
                                       start=True, stop=True)
                    mm.then_inc(s("d_pd"), 1)
                BT = [4, 5, 2, 3]
                for first in (True, False):
                    follow.next("d_dp")
                    if not first:
                        follow.next("d_ap")
                    for n in range(4):
                        for h in range(HG):
                            mm = pe.transpose(bank(BT[n])[:, h * P:(h + 1) * P], r_exp[:, n, h, :], idn)
                        mm.then_inc(s("d_pa"), 1)
                with follow.loop(5, d_ap=3, d_dp=2):
                    warm(1)
                    follow.next("d_ap")
                    for j in range(2):
                        for n in (2 * j, 2 * j + 1):
                            for h in range(HG):
                                o = ((n % 2) * HG + h) * CH
                                mm = pe.matmul(bank(6 + j)[:, o:o + CH], a_exp[:, n, h, :], bmat[:, n, h, :],
                                               start=True, stop=True)
                        mm.then_inc(s("d_pa"), 1)
                    for j in range(2):
                        follow.next("d_ap")
                        for n in (2 * j, 2 * j + 1):
                            for h in range(HG):
                                o = ((n % 2) * HG + h) * CH
                                mm = pe.matmul(bank(2 + j)[:, o:o + CH], t_exp[:, n, h, :], pcs[:, n, h, :],
                                               start=True, stop=True)
                        mm.then_inc(s("d_pd"), 1)
                    for j in range(2):
                        warm(1)
                        follow.next("d_dp")
                        for n in (2 * j, 2 * j + 1):
                            for h in range(HG):
                                mm = pe.transpose(bank(BT[n])[:, h * P:(h + 1) * P], r_exp[:, n, h, :], idn)
                            mm.then_inc(s("d_pa"), 1)
                follow.next("d_ap")
                for n in range(4):
                    p = PAIR[n]
                    if n:
                        for b, base in ((2, HD), (3, 0)):
                            follow.next("d_dp")
                            for h in range(HG):
                                for d in range(2):
                                    side = side_of(n, d)
                                    c = 3 - p if side else p
                                    mm = pe.matmul(bank(b)[SIDES[side], h * P:(h + 1) * P],
                                                   chunk(qkv[:, base + H[h], :], c), st[:, d, h, :],
                                                   start=True, stop=True)
                            mm.then_inc(s("d_pd"), 1)
                    follow.next("d_dp")
                    for h in range(HG):
                        mm = pe.matmul(bank(4)[:, h * P:(h + 1) * P], r_exp[:, n, h, :], rr[:, h, :], start=True, stop=True)
                    mm.then_inc(s("d_pd"), 1)
                    follow.next("d_dp")
                    if n < 3:
                        for h in range(HG):
                            for d in range(2):
                                rows = SIDES[side_of(n, d)]
                                mm = pe.matmul(bank(6 + d)[:, h * P:(h + 1) * P], ktm[rows, p, h, :], vns[rows, h, :],
                                               start=True, stop=True)
                        mm.then_inc(s("d_pd"), 1)
                    follow.next("d_dp")
                    for h in range(HG):
                        mm = pe.matmul(bank(5)[:, h * P:(h + 1) * P], att_exp[:, n, h, :], vn[:, h, :], start=True, stop=True)
                    mm.then_inc(s("d_pd"), 1)
                follow.next("d_dp")
                for p in range(2):
                    for h in range(HG):
                        mm = pe.transpose(bank(2 + p)[:, h * P:(h + 1) * P], oacc[:, p, h, :], idn)
                    mm.then_inc(s("d_pd"), 1)

            def columns(iters, n, hi, lo, ready):
                with cur.repeat(iters, SIX if n == 6 else list(range(4)), range(n), [0, 1] * (n // 2)):
                    for j in range(n):
                        slab(j, j, j, 0, 8, True, True, hi, lo, ready if j == 0 else None)

            def mlp(layer):
                norm()
                columns(4, 4, u_hi, u_lo, (s("u_ready"), 4 * (norm_n[1] - 1)))
                mids = (s("mid_ready"), 22 + 16 * layer)
                for _ in range(1 + layer):
                    with cur.repeat(2 - layer, [0, 1, 2, 3] * 2, range(8), [0, 1]):
                        for j in range(8):
                            slab(j, j, j // 4, 8 * (j % 4), 8, j % 4 == 0, j % 4 == 3, mid_hi, mid_lo, mids)

            def attention():
                norm()
                columns(2, 6, u_hi, u_lo, (s("u_ready"), 4 * (norm_n[1] - 1)))
                for b in range(2):
                    pe.wait_ge(bank_free[b], cur.bank_uses[b])
                for t in range(2):
                    for h in range(8):
                        mm = pe.transpose(bank(2 + 2 * t + h // 4)[:, (h % 4) * P:(h % 4 + 1) * P],
                                          qa[:, 16 + h, t * P:(t + 1) * P], cs("ident"))
                        if h % 4 == 3:
                            mm.then_inc(s("a_vT"), 1)

                def scores(h):
                    if h >= 2:
                        pe.wait_ge(s("a_sread"), h - 1)
                    for blk, (o, n) in enumerate(((256, 128), (0, 256))):
                        for m in range(2):
                            r = slice(64 * m, 64 * m + 64)
                            mm = pe.matmul(bank(2 + 2 * (h % 2) + m)[:, o:o + n], qa[r, h, blk * P:(blk + 1) * P],
                                           qa[r, 8 + h, 0:n], start=True, stop=True)
                    mm.then_inc(s("a_sc"), 1)
                pe.wait_ge(s("a_v"), 1)
                scores(0)
                scores(1)
                for h in range(8):
                    pe.wait_ge(s("a_comb"), h + 1)
                    if h:
                        pe.wait_ge(s("a_aT"), h)
                    for j, o in enumerate((256, 0, 128)):
                        mm = pe.transpose(bank(6)[:, j * P:(j + 1) * P], aa[h % 2][:, o:o + P], cs("ident"))
                    mm.then_inc(s("a_T"), 1)
                    pe.wait_ge(s("a_aT"), h + 1)
                    if h:
                        pe.wait_ge(s("a_o"), h)
                    pe.matmul(bank(7)[:, 0:P], aT[:, 0:P], vt2[:, 0, h, :], start=True, stop=True)
                    pe.matmul(bank(7)[:, P:2 * P], aT[:, P:2 * P], vt2[:, 0, h, :], start=True, stop=False)
                    pe.matmul(bank(7)[:, P:2 * P], aT[:, 2 * P:3 * P], vt2[:, 1, h, :], start=False, stop=True)\
                        .then_inc(s("a_pv"), 1)
                    if h + 2 < 8:
                        scores(h + 2)
                pe.wait_ge(s("a_on"), 1)
                for h in range(8):
                    for t in range(2):
                        mm = pe.transpose(bank(2 + h // 2)[:, (h % 2) * S + t * P:(h % 2) * S + (t + 1) * P],
                                          otm[:, t, h, :], cs("ident"))
                    if h % 2:
                        mm.then_inc(s("a_oT"), 1)
                columns(1, 4, u_hi, u_lo, (s("a_ready"), 0))

            def mlstm():
                norm()
                base = 4 * (norm_n[1] - 1)
                pe.wait_ge(s("u_ready"), base + 4)
                for g in range(2):
                    for kt in range(KD):
                        mm = pe.matmul(bank(3)[0:4, g * S:(g + 1) * S], wg2[:, kt, 4 * g:4 * g + 4], uf[:, kt, :],
                                       start=(kt == 0), stop=(kt == KD - 1))
                mm.then_inc(s("m_gates"), 1)
                columns(1, 4, u_hi, u_lo, None)
                columns(2, 4, u_hi, u_lo, None)
                pe.wait_ge(s("m_rows"), 1)
                for t in range(2):
                    mm = pe.transpose(bank(2)[:, 4 * t:4 * t + 4], rows2[0:4, 4, t * P:(t + 1) * P], cs("ident")[0:4, 0:4])
                mm.then_inc(s("m_acol"), 1)
                for b in range(2):
                    pe.wait_ge(bank_free[b], cur.bank_uses[b])
                for t in range(2):
                    for k in range(8):
                        mm = pe.transpose(bank(4 + 2 * t + k // 4)[:, (k % 4) * P:(k % 4 + 1) * P],
                                          vo[:, k, t * P:(t + 1) * P], cs("ident"))
                        if k % 4 == 3:
                            mm.then_inc(s("m_vT"), 1)
                pe.wait_ge(s("m_qk"), 4)

                def head(h):
                    if h:
                        pe.wait_ge(s("m_bcread"), h)
                    pe.matmul(bank(2), cs2("sel")[0:4, h * P:(h + 1) * P],
                              rows2[0:4, 6:8, :].rearrange("q a t -> q (a t)"), start=True, stop=True)
                    pe.matmul(bank(3)[:, 0:S], qk2[:, 4 + h, 0:P], qk2[:, h, :], start=True, stop=True)
                    pe.matmul(bank(3)[:, S:S + P], qk2[:, 4 + h, P:S], qk2[:, h, P:S], start=True, stop=True)\
                        .then_inc(s("m_s"), 1)
                pe.wait_ge(s("m_v"), 1)
                pe.wait_ge(s("m_acol_in"), 1)
                head(0)
                for h in range(ML_H):
                    pe.wait_ge(s("m_sc"), h + 1)
                    if h:
                        pe.wait_ge(s("m_y"), h)
                    for m in range(2):
                        pe.matmul(bank(4)[:, m * S:(m + 1) * S], vt3[:, 0, 2 * h + m, :], sct[:, 0:S], start=True, stop=False)
                        pe.matmul(bank(4)[:, m * S + P:(m + 1) * S], vt3[:, 1, 2 * h + m, :], sct[:, S:S + P],
                                  start=False, stop=True)
                    pe.matmul(bank(5)[:, 0:S], cs("ones"), sct[:, 0:S], start=True, stop=False)
                    pe.matmul(bank(5)[:, P:S], cs("ones"), sct[:, S:S + P], start=False, stop=True)\
                        .then_inc(s("m_num"), 1)
                    pe.wait_ge(s("m_nsq"), h + 1)
                    for m in range(2):
                        mm = pe.matmul(bank(6)[:, 0:S], cs("ones"), nsq[:, m, :], start=(m == 0), stop=(m == 1))
                    mm.then_inc(s("m_ss"), 1)
                    if h + 1 < ML_H:
                        head(h + 1)
                columns(1, 4, u_hi, u_lo, (s("m_ready"), 0))

            ffn(True, 0)
            norm(meanwhile=mixer_mods)
            mixer()
            ffn(False, 11)
            norm(False)
            attention()
            mlp(0)
            mlstm()
            mlp(1)
            norm(False)
            pe.wait_ge(s("u_out"), 1)
            for k in range(KD):
                for t in range(2):
                    mm = pe.transpose(bank(3 + t * 2 + k // 4)[:, (k % 4) * P:(k % 4 + 1) * P],
                                      uf[:, k, t * P:(t + 1) * P], cs("ident"))
            mm.then_inc(s("y_T"), 1)

        @block.scalar
        def _(act):
            chain = Chain(act, s("act_order"))
            cur = Cursor(act, chain)
            rows = []
            for n, a in (("ffn1", A["norm_ffn1"][0]), ("mix", A["norm_mix"][0]), ("ffn2", A["norm_ffn2"][0]),
                         ("final", A["norm_final"]), ("attn", A["attn_norm_2"][0]), ("mlstm", A["mlstm_norm_2"][0]),
                         ("final2", A["final_norm_2"])):
                rows.append((0, NRM[n], 8, a.rearrange("(r c) -> r c", c=P)))
            rows.append((0, NRM["mlp"], 16, A["mlp_norm_2"].rearrange("l (r c) -> (l r) c", c=P)))
            rows.append((0, DN_NORM, 1, A["dn_norm"]))
            rows.append((0, SUBLN, 1, A["attn_subln_2"]))
            rows.append((0, HEAD_NORM, 8, A["mlstm_head_norm_2"][0].rearrange("(r c) -> r c", c=P)))
            rows.append((0, CONV2, 32, A["mlstm_conv_w_2"][0].rearrange("t (r c) -> (t r) c", c=P)))
            rows.append((0, CONV2_B, 8, A["mlstm_conv_b_2"][0].rearrange("(r c) -> r c", c=P)))
            rows.append((1, 0, 72, A["b_ada"][0].rearrange("(r c) -> r c", c=P)))
            rows.append((1, CONV_A - P, 12, A["conv_a"][0].rearrange("t (r c) -> (t r) c", c=P)))
            rows.append((2, 0, 120, A["conv_dn"][0].rearrange("t (r c) -> (t r) c", c=P)))
            act.dma_start(cact, A["c"].rearrange("a (k p) -> p (a k)", p=P)).then_inc(s("c_in"), 16)
            act.dma_start(x_tm, A["x"][0].rearrange("(t p) d -> p t d", p=P)).then_inc(s("x_in"), 16)
            for j, r, n, a in rows[:4]:
                act.dma_start(prow[r:r + n, j, :], a).then_inc(s("params_in"), 16)
            act.wait_ge(s("c_in"), 16)
            act.activation(cact, cact, ACT.Silu).then_inc(s("c_ready"), 1)
            for j, r, n, a in rows[4:]:
                act.dma_start(prow[r:r + n, j, :], a).then_inc(s("params_in"), 16)
            for j, n in enumerate(("a_log_fwd", "a_log_bwd", "dt_bias_fwd", "dt_bias_bwd")):
                act.dma_start(abc[:, j, :], A[n].broadcast_to([P, HD])).then_inc(s("abc_in"), 16)
            assert len(rows) == NPAR, len(rows)
            act.dma_start(onehot, A["consts2"][:, 0:384]).then_inc(s("bias_in"), 16)
            act.dma_start(relt[0:BUCKETS, :], A["rel_bias_2"]).then_inc(s("bias_in"), 16)
            for j, n in enumerate(("q1", "q2", "k1", "k2")):
                act.dma_start(lamv[:, j, :], A[f"attn_lambda_{n}_2"].broadcast_to([P, 64])).then_inc(s("small_in"), 16)
            act.dma_start(bif[:, 0:1], A["mlstm_b_i_2"].rearrange("a h -> h a")).then_inc(s("small_in"), 16)
            act.dma_start(bif[:, 1:2], A["mlstm_b_f_2"].rearrange("a h -> h a")).then_inc(s("small_in"), 16)
            act.dma_start(wg2, A["mlstm_w_in_2"][0].rearrange("(k p) n -> p k n", p=P)[:, :, 3072:3080])\
                .then_inc(s("small_in"), 16)

            act.wait_ge(s("abc_in"), 64)
            act.wait_ge(s("c_ready"), 1)
            chain.link(act.copy(act_mark, cact[:, 0:1]))
            with cur.repeat(2, [0, 1, 2, 3], [], []):
                for j in HEAD_POOL:
                    r, k = cur.use(j)
                    arrived(act, r, k)
                    for kt in range(KD):
                        op = act.activation(raw[r][:, kt, :], raw[r][:, kt, :], ACT.Copy, scale=cact[:, kt:kt + 1])
                    op.then_inc(s("ada_scaled"), 1)
            act.wait_ge(s("brow_ps"), 1)
            chain.link(act.copy(brow, bank(7)[0:8, 0:384]))
            act.dma_start(bias_dram, brow[:, None, :].broadcast_to([8, P, 384])).then_inc(s("brow_out"), 16)
            act.wait_ge(s("small_in"), 16 * 7)
            act.wait_ge(s("x_T"), 1)
            for b in range(4):
                mm = act.copy(hT[:, 2 * b:2 * b + 2, :], bank(3 + b).rearrange("p (k t) -> p k t", k=2))
            mm.then_inc(s("h_ready"), 1)

            def split_hi(r, k, u):
                arrived(act, r, k)
                for h in range(2):
                    act.wait_ge(halves_free, u + (h + 1))
                    half = (cur.stat + h) % HALVES
                    act.copy(w_hi[half], raw[r][:, 4 * h:4 * h + 4, :]).then_inc(hi_ready, 1)

            def walk(iters, slots, splits, banks, hook, links=0, last=False):
                with cur.repeat(iters, slots, splits, banks, links) as i:
                    for n in range(len(splits)):
                        r, k, u = cur.next_split(n)
                        if not (last and n == len(splits) - 1):
                            cur.stat = cur.half + 2 * (n + 1)
                            split_hi(r, k, u)
                        hook(i, n)

            norm_n = [0, 0]

            def norm(final=False):
                n = norm_n[0] = norm_n[0] + 1
                act.wait_ge(s("ss_ready"), n)
                act.activation(rms, bank(2)[:, 0:S], ACT.Sqrt, scale=1.0 / D, bias=cc[:, 0:1]).then_inc(s("rms_ready"), 1)
                if final:
                    return
                norm_n[1] += 1
                for c in range(4):
                    act.wait_ge(s("uf_ready"), 4 * (norm_n[1] - 1) + c + 1)
                    act.copy(u_hi[:, 2 * c:2 * c + 2, :], uf[:, 2 * c:2 * c + 2, :])\
                        .then_inc(s("u_hi_ready"), 1)

            cur.stat = 0
            act.wait_ge(s("mod_head"), 1)
            act.wait_ge(s("brow_out"), 16)
            split_hi(0, cur.slot_uses[0], 0)

            def ffn(with_ada, base):
                norm()

                def up(i, n):
                    if n == 0:
                        act.wait_ge(halves_free, cur.half_of(0) + (HALVES + 2))
                        act.activation(sil, bank(0).rearrange("p (k t) -> p k t", k=2), ACT.Silu)\
                            .then_inc(bank_free[0], 1)
                    else:
                        act.wait_ge(bank_free[1], cur.bank_use(1)[1] + 1)
                        act.copy(mid_hi[:, bass.ds(i * 2, 2), :], mt).then_inc(s("mid_hi_ready"), 1)
                walk(11, [0, 1, 2] if with_ada else [0, 1], [0, 1], [0, 1], up)
                if with_ada:
                    cur.skip(1, [3], [], [])
                slots = DOWN_ADA if with_ada else [0, 1, 2] * 2
                splits = DOWN_SPLIT if with_ada else list(range(6))
                walk(2, slots, splits, [0, 1], lambda i, n: None,
                     last=False)

            follow = Follow(act, s)
            link = chain.link

            def evict(g, n, dst):
                b, uses = cur.bank_use(g)
                act.wait_ge(halves_free, cur.half_of(n) + (HALVES + 2))
                act.copy(dst, bank(b).rearrange("p (k t) -> p k t", k=2)).then_inc(bank_free[b], 1)

            def mixer():
                norm()
                act.wait_ge(s("pads_zero"), 1)
                act.wait_ge(s("ba_ps"), 1)
                act.activation(tk(TB).rearrange("p (a b) -> p a b", a=2),
                               bank(3)[:, 0:64].rearrange("p (a b) -> p a b", a=2)[:, :, 0:16], ACT.Sigmoid)\
                    .then_inc(s("beta_ready"), 1)
                act.activation(tk(TE, 16), abc[:, 0:2, :].rearrange("p a b -> p (a b)"), ACT.Exp)\
                    .then_inc(s("silu_done"), 2)
                act.wait_ge(s("sp_abs"), 1)
                link(act.activation(tk(TAB), tk(TAB), ACT.Exp, scale=-1.0))
                act.activation(tk(TAB), tk(TAB), ACT.Ln, bias=cc[:, 2:3]).then_inc(s("sp_ln"), 1)
                walk(1, SIX, range(6), [0, 1] * 3, lambda i, n: evict(n, n, ca[:, 2 * n:2 * n + 2, :]))
                act.wait_ge(s("g_ps"), 1)
                act.copy(tk(TGS), bank(4)[:, 0:32]).then_inc(s("gs_ready"), 1)
                act.activation(tk(TEG), bank(4)[:, 0:32], ACT.Exp)
                act.activation(tok[:, TES:TES + 2, :], bank(4)[:, 64:128].rearrange("p (a b) -> p a b", a=2), ACT.Exp)\
                    .then_inc(s("eg_ready"), 1)
                act.wait_ge(s("dg_ready"), 1)
                act.activation(tk(TED), tk(TED), ACT.Exp).then_inc(s("eg_ready"), 1)

                def conv(i, n):
                    def silu(m):
                        act.wait_ge(s("conv_done"), i * 6 + (m + 3))
                        for p in range(2):
                            x = cacc[m % 2].rearrange("q k (c t) -> q k c t", c=4)[:, :, p:4 - p:3 - 2 * p, :]
                            y = qkv[:, bass.ds(i * 12 + 2 * m, 2), p * P:(p + 1) * P]
                            op = act.activation(y.rearrange("q k (c t) -> q k c t", c=2), x, ACT.Silu)
                        op.then_inc(s("silu_done"), 1)
                    act.wait_ge(s("conv_done"), i * 6 + (n + 1))
                    evict(n, n, pad[n % 2][:, :, 2:2 + S])
                    if n:
                        silu(n - 1)
                    if n == 5:
                        silu(5)
                walk(2, SIX, range(6), [0, 1] * 3, conv)
                act.wait_ge(s("yaf_ready"), 1)
                act.copy(ya_hi, yaf).then_inc(s("ya_hi_ready"), 1)

                def zg(i, n):
                    b, uses = cur.bank_use(n)
                    act.wait_ge(halves_free, cur.half_of(n) + (HALVES + 2))
                    if n < 2:
                        dst, f = zs[:, bass.ds(i * 4 + 2 * n, 2), :], ACT.Silu
                    else:
                        dst, f = gt[:, bass.ds(i * 8 + 2 * (n - 2), 2), :], ACT.Sigmoid
                    act.activation(dst, bank(b).rearrange("p (k t) -> p k t", k=2), f).then_inc(bank_free[b], 1)
                walk(2, ZG, ZG_SPLIT, [0, 1] * 3, zg)
                walk(1, [0, 1], [0, 1], [0, 1, 0, 1], lambda i, n: None)
                for hh in range(HD // HG):
                    delta(hh)
                for c in range(2):
                    follow.next("d_da")
                    act.copy(u_hi[:, 4 * c:4 * c + 4, :], qkv[:, 4 * c:4 * c + 4, :]).then_inc(s("yb_hi_ready"), 1)

                def merge(i, n):
                    act.wait_ge(s("mg_f"), n + 1)
                    act.copy(mg_hi[:, 2 * n:2 * n + 2, :], gt[:, 2 * n:2 * n + 2, :]).then_inc(s("mg_hi_ready"), 1)
                walk(1, [0, 1, 2, 3], range(4), [0, 1] * 2, merge)
                walk(1, [0, 1, 2, 3], range(4), [0, 1] * 2, lambda i, n: None)

            def delta(hh):
                def b4(i):
                    return bank(i).rearrange("p (h c) -> p h c", h=HG)
                for t, x in enumerate((ktm, qtm, vtm)):
                    for p in range(2):
                        follow.next("d_pa")
                        op = act.copy(x[:, p, :, :], b4(2 + 2 * t + p))
                        if t < 2 or p == 1:
                            op.then_inc(s("d_ad"), 1)
                follow.next("d_da")
                act.activation(tk(TE, 16), tk(TX, 16), ACT.Sqrt, bias=cc[:, 0:1]).then_inc(s("d_ad"), 1)
                for t, base in enumerate((HD, 0)):
                    for p in range(2):
                        follow.next("d_pa")
                        lo = base + hh * HG
                        act.copy(qkv[:, lo:lo + HG, p * P:(p + 1) * P], b4(2 + 2 * t + p)).then_inc(s("d_ap"), 1)
                follow.next("d_pa")
                for j in range(2):
                    op = act.copy(kk[:, j].rearrange("q p h c -> q (p h c)"), bank(6 + j))
                op.then_inc(s("d_ad"), 1)
                follow.next("d_da")
                act.activation(dec, dec, ACT.Exp).then_inc(s("d_ad"), 1)
                BT = [4, 5, 2, 3]
                for n in range(4):
                    follow.next("d_pa")
                    if n < 3:
                        act.copy(a_exp[:, n], b4(BT[n]))
                    else:
                        act.copy(a_exp[:, n, 0:2], b4(BT[n])[:, 0:2]).then_inc(s("d_ad"), 1)
                        act.copy(a_exp[:, n, 2:4], b4(BT[n])[:, 2:4]).then_inc(s("d_ap"), 1)

                def t_copies():
                    for n in range(4):
                        follow.next("d_pa")
                        op = act.copy(t_exp[:, n], b4(BT[n]))
                    op.then_inc(s("d_ap"), 1)
                t_copies()
                with follow.loop(5, d_pa=6):
                    for j in range(2):
                        follow.next("d_pa")
                        act.copy(pcs[:, 2 * j:2 * j + 2].rearrange("q n h c -> q (n h c)"), bank(6 + j))\
                            .then_inc(s("d_ap"), 1)
                    t_copies()
                follow.next("d_da")
                act.activation(tk(TE, 8), tk(TX, 8), ACT.Sqrt, bias=cc[:, 0:1], scale=1.0 / P).then_inc(s("d_ad"), 1)

            def columns(iters, n, hook, last=False):
                walk(iters, SIX if n == 6 else list(range(4)), range(n), [0, 1] * (n // 2), hook)

            idle = lambda i, n: None

            def two(b):
                return bank(b).rearrange("p (k t) -> p k t", k=2)

            def mlp(layer):
                norm()

                def up(i, n):
                    b, uses = cur.bank_use(n)
                    r = (sil, sil2)[n % 2]
                    act.wait_ge(halves_free, cur.half_of(n) + (HALVES + 2))
                    act.wait_ge(s("mid_ready"), i * 4 + (22 + 16 * layer + n - 1))
                    act.activation(r, two(b), ACT.Relu).then_inc(bank_free[b], 1)
                    act.wait_ge(bank_free[b], uses + 1)
                    act.activation(mid_hi[:, bass.ds(i * 8 + 2 * n, 2), :], r, ACT.Square)\
                        .then_inc(s("mid_hi_ready"), 1)
                columns(4, 4, up)
                if layer == 0:
                    walk(2, [0, 1, 2, 3] * 2, range(8), [0, 1], idle)
                else:
                    walk(1, [0, 1, 2, 3] * 2, range(8), [0, 1], idle)
                    walk(1, [0, 1, 2, 3] * 2, range(8), [0, 1], idle, last=True)

            def attention():
                norm()
                act.dma_start(tz[:, :, 0:S], bass.AP(tensor=bias_dram.tensor, offset=P - 1,
                                                     ap=[[384 - 1, P], [384 * P, 8], [1, S]]))\
                    .then_inc(s("tz_in"), 16)
                act.wait_ge(s("a_lam"), 1)
                act.activation(lam[:, 2:4], lam[:, 0:2], ACT.Exp).then_inc(s("a_elam"), 1)
                columns(2, 6, lambda i, n: evict(n, n, qa[:, bass.ds(i * 12 + 2 * n, 2), :]))
                for j in range(4):
                    act.wait_ge(s("a_vT"), j + 1)
                    op = act.copy(vt2[:, j // 2, 4 * (j % 2):4 * (j % 2) + 4, :], bank(2 + j).rearrange("p (h c) -> p h c", h=4))
                op.then_inc(s("a_v"), 1)

                def exps(h):
                    act.wait_ge(s("a_max"), h + 1)
                    x = sc2[h % 2]
                    for m in range(2):
                        for blk, (o, n) in enumerate(((256, 128), (0, 256))):
                            c = 2 * m + blk
                            op = act.activation(x[:, m, o:o + n], x[:, m, o:o + n], ACT.Exp,
                                                bias=stat[:, 4 * (h % 2) + c:4 * (h % 2) + c + 1],
                                                accum_out=stat[:, 8 + 4 * (h % 2) + c:9 + 4 * (h % 2) + c])
                    op.then_inc(s("a_exp"), 1)
                exps(0)
                for h in range(8):
                    if h < 7:
                        exps(h + 1)
                    act.wait_ge(s("a_T"), h + 1)
                    act.copy(aT, bank(6)[:, 0:384]).then_inc(s("a_aT"), 1)
                    act.wait_ge(s("a_pv"), h + 1)
                    act.copy(otm[:, :, h, :], bank(7)[:, 0:S].rearrange("p (t c) -> p t c", t=2)).then_inc(s("a_o"), 1)
                act.wait_ge(s("a_ss"), 1)
                act.activation(stat[:, 16:32], stat[:, 16:32], ACT.Sqrt, bias=cc[:, 0:1], scale=1.0 / P)\
                    .then_inc(s("a_rms"), 1)
                for b in range(4):
                    act.wait_ge(s("a_oT"), b + 1)
                    x = uf[:, 2 * b:2 * b + 2, :]
                    link(act.activation(x, two(2 + b), ACT.Copy, scale=lam[:, 6:7]))
                    act.copy(u_hi[:, 2 * b:2 * b + 2, :], x).then_inc(s("a_uhi"), 1)
                columns(1, 4, idle)

            def mlstm():
                norm()
                act.wait_ge(s("m_x"), 1)
                link(act.activation(rows2[:, 2, :], rows2[:, 2, :], ACT.Exp, scale=-1.0))
                act.activation(rows2[:, 2, :], rows2[:, 2, :], ACT.Ln, bias=cc[0:4, 2:3]).then_inc(s("m_ln"), 1)

                def conv(i, n):
                    def silu(m):
                        act.wait_ge(s("m_conv"), m + 1)
                        for k in range(2):
                            t = 2 * m + k
                            op = act.activation(qk2[:, t, :], cac2[m % 2][:, k, :], ACT.Silu,
                                                bias=prm[:, CONV2_B + t:CONV2_B + t + 1])
                        op.then_inc(s("m_qk"), 1)
                    if n == 0:
                        act.wait_ge(s("m_pads"), 1)
                    if n >= 2:
                        act.wait_ge(s("m_conv"), n - 1)
                    evict(n, n, pad2[n % 2][:, :, 3:3 + S])
                    if n:
                        silu(n - 1)
                    if n == 3:
                        silu(3)
                columns(1, 4, conv)
                act.wait_ge(s("m_m"), 1)
                act.activation(rows2[:, 7, :], rows2[:, 7, :], ACT.Exp, scale=-1.0).then_inc(s("m_rows"), 1)
                columns(2, 4, lambda i, n: evict(n, n, vo[:, bass.ds(i * 8 + 2 * n, 2), :]))
                act.wait_ge(s("m_acol"), 1)
                act.copy(acol, bank(2)[:, 0:8].rearrange("p (t h) -> p t h", t=2)).then_inc(s("m_acol_in"), 1)
                for j in range(4):
                    act.wait_ge(s("m_vT"), j + 1)
                    op = act.copy(vt3[:, j // 2, 4 * (j % 2):4 * (j % 2) + 4, :], bank(4 + j).rearrange("p (h c) -> p h c", h=4))
                op.then_inc(s("m_v"), 1)
                act.activation(vo[:, 8:16, :], vo[:, 8:16, :], ACT.Sigmoid).then_inc(s("m_o"), 1)
                for h in range(ML_H):
                    act.wait_ge(s("m_d"), h + 1)
                    act.activation(ex2[:, 0:S], ex2[:, 0:S], ACT.Exp, bias=acol[:, 0, h:h + 1])
                    act.activation(ex2[:, S:S + P], ex2[:, S:S + P], ACT.Exp, bias=acol[:, 1, h:h + 1])\
                        .then_inc(s("m_e"), 1)
                    act.wait_ge(s("m_num"), h + 1)
                    act.activation(nsq, two(4), ACT.Square).then_inc(s("m_nsq"), 1)
                    act.activation(dn, bank(5)[:, 0:S], ACT.Abs).then_inc(s("m_den"), 1)
                    act.wait_ge(s("m_r2"), h + 1)
                    act.activation(rt, rt, ACT.Sqrt).then_inc(s("m_rms"), 1)
                    act.wait_ge(s("m_uf"), h + 1)
                    act.copy(u_hi[:, 2 * h:2 * h + 2, :], uf[:, 2 * h:2 * h + 2, :]).then_inc(s("m_uhi"), 1)
                columns(1, 4, idle)

            ffn(True, 0)
            mixer()
            ffn(False, 11)
            norm(final=True)
            attention()
            mlp(0)
            mlstm()
            mlp(1)
            norm(final=True)
            act.wait_ge(s("y_T"), 1)
            for t in range(2):
                for b in range(2):
                    mm = act.copy(x_tm[:, t, 512 * b:512 * b + 512], bank(3 + 2 * t + b))
            mm.then_inc(s("y_ready"), 1)

        @block.vector
        def _(dve):
            chain = Chain(dve, s("dve_order"))
            link = chain.link
            cur = Cursor(dve, chain)
            for r in range(SLOTS):
                dve.memset(lam[:, r:r + 1], 0.0).then_inc(slab_taken[r], 2)
            dve.memset(cc[:, 0:1], EPS).then_inc(bank_free[0], 1)
            dve.memset(cc[:, 1:2], 0.0).then_inc(bank_free[1], 1)
            dve.memset(cc[:, 2:3], 1.0)
            def split_lo(r, k, u):
                dve.wait_ge(hi_ready, u + 1)
                half = cur.stat % HALVES
                dve.tensor_tensor(w_lo[half], raw[r][:, 0:4, :], w_hi[half].bitcast(F32),
                                  ALU.subtract).then_inc(lo_ready[0], 1)
                dve.memset(marks[:, r:r + 1], 0.0).then_inc(slab_taken[r], 1)

            def walk(iters, slots, splits, banks, hook, links=0, last=False):
                with cur.repeat(iters, slots, splits, banks, links) as i:
                    for n in range(len(splits)):
                        r, k, u = cur.next_split(n)
                        if not (last and n == len(splits) - 1):
                            cur.stat = cur.half + 2 * (n + 1)
                            split_lo(r, k, u)
                        hook(i, n)

            def mod_cols(a, b, src):
                link(dve.tensor_tensor(modc[:, a:b], src, prm[:, B_ADA + a:B_ADA + b], ALU.add))

            norm_n = [0, 0]

            def norm(gain, mod=None, final=False, dst=uf):
                n = norm_n[0] = norm_n[0] + 1
                norm_n[1] += not final
                link(dve.memset(cc[:, 3:4], 0.0))
                for c in range(2):
                    sl = slice(4 * c, 4 * c + 4)
                    dve.tensor_tensor(uf[:, sl, :], hT[:, sl, :], hT[:, sl, :], ALU.mult).then_inc(s("sq_ready"), 1)
                if mod == 24:
                    dve.wait_ge(s("mod_ps"), 3)
                    mod_cols(24, 40, bank(7)[:, 0:16])
                if mod is not None:
                    link(dve.scalar_tensor_tensor(gcol[:, 0:KD], modc[:, mod + KD:mod + 2 * KD], 1.0,
                                                  prm[:, gain:gain + KD], ALU.add, ALU.mult))
                dve.wait_ge(s("rms_ready"), n)
                link(dve.reciprocal(rstd, rms))
                for c in range(4):
                    sl = slice(2 * c, 2 * c + 2)
                    link(dve.tensor_tensor(uf[:, sl, :], hT[:, sl, :],
                                           rstd[:, None, :].broadcast_to([P, 2, S]), ALU.mult))
                    for k in range(2 * c, 2 * c + 2):
                        sc = gcol[:, k:k + 1] if mod is not None else prm[:, gain + k:gain + k + 1]
                        sh = modc[:, mod + k:mod + k + 1] if mod is not None else cc[:, 1:2]
                        last = dve.tensor_scalar(dst[:, k, :], uf[:, k, :], sc, sh, ALU.mult, ALU.add)
                    if not final:
                        last.then_inc(s("uf_ready"), 1)
                        dve.wait_ge(s("u_hi_ready"), 4 * (norm_n[1] - 1) + c + 1)
                        dve.tensor_tensor(u_lo[:, sl, :], uf[:, sl, :], u_hi[:, sl, :].bitcast(F32), ALU.subtract)\
                            .then_inc(s("u_ready"), 1)
                if final and dst is uf:
                    last.then_inc(s("u_out"), 1)

            def ada(j, col, to=acc):
                r, k = cur.use(j)
                dst = to[:, bass.ds(col, SLAB)]
                arrived(dve, r, k)
                for kt in range(KD):
                    op = (dve.scalar_tensor_tensor(dst, raw[r][:, kt, :], cact[:, kt:kt + 1], dst, ALU.mult, ALU.add)
                          if kt else dve.tensor_scalar(dst, raw[r][:, 0, :], cact[:, 0:1], None, ALU.mult))
                    if kt < KD - 1:
                        link(op)
                    else:
                        op.then_inc(slab_taken[r], 2)

            dve.wait_ge(s("c_ready"), 1)
            with cur.repeat(2, [0, 1, 2, 3], [], [], 7 * len(HEAD_DVE)) as i:
                for j in HEAD_DVE:
                    ada(j, i * 1024 + j * SLAB)
            dve.memset(cc[:, 3:4], 0.0).then_inc(s("ada_done"), 2 * len(HEAD_DVE))
            dve.wait_ge(s("prm_T"), 1)
            dve.tensor_copy(prm[:, 0:ROWS1], bank(2)[:, 0:ROWS1])
            dve.tensor_copy(prm[:, P:P + ROWS2], bank(2)[:, P:P + ROWS2])
            link(dve.tensor_copy(prm[:, 2 * P:2 * P + ROWS3], bank(2)[:, 2 * P:2 * P + ROWS3]))
            dve.wait_ge(s("mod_ps"), 1)
            dve.wait_ge(s("h_ready"), 1)
            mod_cols(0, 16, bank(7)[:, 0:16])
            dve.memset(cc[:, 3:4], 0.0).then_inc(s("mod_head"), 1)
            cur.stat = 0
            split_lo(0, cur.slot_uses[0], 0)

            def residual(g, t, gate):
                b, uses = cur.bank_use(g)
                dve.wait_ge(halves_free, cur.done)
                for m in range(2):
                    x = hT[:, bass.ds(t + m, 1), :]
                    last = dve.scalar_tensor_tensor(x, bank(b)[:, None, m * S:(m + 1) * S],
                                                    gcol[:, bass.ds(t + m + gate, 1)], x, ALU.mult, ALU.add)
                last.then_inc(bank_free[b], 1)

            def ffn(with_ada, gain, mod, gate, base):
                norm(gain, mod)

                def up(i, n):
                    if n == 0 and with_ada:
                        ada(2, i * SLAB + 8 * SLAB)
                    if n == 1:
                        dve.wait_ge(halves_free, cur.half_of(1) + (HALVES + 2))
                        dve.wait_ge(bank_free[0], cur.bank_use(0)[1] + 1)
                        dve.tensor_tensor(mt, sil, bank(1).rearrange("p (k t) -> p k t", k=2), ALU.mult)\
                            .then_inc(bank_free[1], 1)
                        dve.wait_ge(s("mid_hi_ready"), i + (base + 1))
                        dve.tensor_tensor(mid_lo[:, bass.ds(i * 2, 2), :], mt,
                                          mid_hi[:, bass.ds(i * 2, 2), :].bitcast(F32), ALU.subtract)\
                            .then_inc(s("mid_ready"), 1)
                walk(11, [0, 1, 2] if with_ada else [0, 1], [0, 1], [0, 1], up, 7 if with_ada else 0)
                if with_ada:
                    dve.memset(cc[:, 3:4], 0.0).then_inc(s("ada_done"), 11)
                    with cur.repeat(1, [3], [], []):
                        ada(0, 19 * SLAB)
                    dve.wait_ge(s("mod_ps"), 2)
                    mod_cols(16, 24, bank(7)[:, 0:8])
                link(dve.tensor_scalar(gcol[:, KD:2 * KD], modc[:, gate:gate + KD], 0.5, None, ALU.mult))
                slots = DOWN_ADA if with_ada else [0, 1, 2] * 2
                splits = DOWN_SPLIT if with_ada else list(range(6))

                def down(i, n):
                    if n % 3 == 2:
                        cur.done = cur.half_of(n) + (HALVES + 2)
                        residual(n // 3, i * 4 + 2 * (n // 3), KD)
                    if n % 3 == 1 and with_ada:
                        for q in range(2):
                            ada(5 * (n // 3) + 3 + q, i * (4 * SLAB) + (20 + 2 * (n // 3) + q) * SLAB)
                walk(2, slots, splits, [0, 1], down, 28 if with_ada else 0)
                if with_ada:
                    dve.memset(lam[:, 4:5], 0.0).then_inc(s("ada_done"), 9)

            follow = Follow(dve, s)
            mul, add, sub = ALU.mult, ALU.add, ALU.subtract

            def mixer():
                norm(NRM["mix"], 24)
                dve.wait_ge(s("mod_ps"), 4)
                mod_cols(40, 56, bank(6)[:, 0:16])
                for b in pad:
                    dve.memset(b[:, :, 0:2], 0.0)
                    dve.memset(b[:, :, S + 2:S + 4], 0.0)
                dve.memset(cv[:, :, 0:1], 0.0)
                dve.memset(cv[:, :, S + 1:S + 2], 0.0).then_inc(s("pads_zero"), 1)
                dve.memset(cc[:, 3:4], 0.0).then_inc(s("conv_done"), 2)
                dve.wait_ge(s("ba_ps"), 1)
                dve.wait_ge(s("beta_ready"), 1)
                v2 = lambda r: tk(r).rearrange("p (a b) -> p a b", a=2)
                link(dve.tensor_tensor(v2(TX), bank(3)[:, 0:64].rearrange("p (a b) -> p a b", a=2)[:, :, 16:32],
                                       abc[:, None, 2:4, :].rearrange("p o a b -> p o (a b)").broadcast_to([P, 2, 16]), add))
                dve.scalar_tensor_tensor(tk(TAB), tk(TX), -1.0, tk(TX), mul, ALU.max).then_inc(s("sp_abs"), 1)
                dve.wait_ge(s("sp_ln"), 1)
                link(dve.scalar_tensor_tensor(tk(TX), tk(TX), 0.0, tk(TAB), ALU.max, add))
                link(dve.scalar_tensor_tensor(v2(TG), v2(TX), -1.0, tok[:, TE:TE + 1, 0:16].broadcast_to([P, 2, 16]),
                                              mul, mul))
                for src, dst in ((TG, TGN), (TB, TBN)):
                    for side, rows in enumerate(SIDES):
                        x = tok[rows, src, :].rearrange("q (p d h) -> q p d h", p=2, d=2)
                        y = tok[rows, dst, :].rearrange("q (n h) -> q n h", n=4)
                        dve.tensor_copy(y[:, 0:2, :], x[:, :, side, :])
                        dve.tensor_copy(y[:, 2, :], x[:, 1, 1 - side, :])
                        last = dve.tensor_copy(y[:, 3, :], x[:, 0, 1 - side, :])
                last.then_inc(s("g_ready"), 1)
                walk(1, SIX, range(6), [0, 1] * 3, lambda i, n: None)
                dve.wait_ge(s("gs_ready"), 1)
                dve.wait_ge(s("eg_ready"), 1)
                dve.tensor_tensor(tk(TED), bank(4)[:, 32:64], tk(TGS), sub).then_inc(s("dg_ready"), 1)
                dve.wait_ge(s("eg_ready"), 2)
                link(dve.tensor_tensor(tk(TAB), tk(TBN), tk(TEG), mul))

                def conv(i, n):
                    b, uses = cur.bank_use(n)
                    dve.wait_ge(bank_free[b], uses + 1)
                    dve.wait_ge(s("silu_done"), i * 6 + (n + 1))
                    for t in range(5):
                        for m in range(2):
                            w = prm[:, bass.ds(i * 12 + (CONV_DN + 24 * t + 2 * n + m), 1)]
                            x, y = pad[n % 2][:, m, t:t + S], cacc[n % 2][:, m, :]
                            if t == 0:
                                op = dve.tensor_scalar(y, x, w, None, mul)
                            else:
                                op = dve.scalar_tensor_tensor(y, x, w, y, mul, add)
                            if t == 4 and m == 1:
                                op.then_inc(s("conv_done"), 1)
                            elif m == 1:
                                link(op)
                walk(2, SIX, range(6), [0, 1] * 3, conv, 24)
                link(dve.tensor_tensor(cv[:, :, 1:1 + S], ca[:, 4:8, :], ca[:, 8:12, :], mul))
                for t in range(3):
                    for m in range(4):
                        w = prm[:, CONV_A + 4 * t + m:CONV_A + 4 * t + m + 1]
                        x = cv[:, m, t:t + S]
                        op = (dve.tensor_scalar(yaf[:, m, :], x, w, None, mul) if t == 0 else
                              dve.scalar_tensor_tensor(yaf[:, m, :], x, w, yaf[:, m, :], mul, add))
                    link(op)
                dve.tensor_tensor(yaf, yaf, ca[:, 0:4, :], mul).then_inc(s("yaf_ready"), 1)
                dve.wait_ge(s("ya_hi_ready"), 1)
                dve.wait_ge(s("silu_done"), 14)
                dve.tensor_tensor(ya_lo, yaf, ya_hi.bitcast(F32), sub).then_inc(s("ya_ready"), 1)

                def zg(i, n):
                    if n < 4:
                        ada(2 * n + 2, i * (4 * SLAB) + n * SLAB, acc8)
                walk(2, ZG, ZG_SPLIT, [0, 1] * 3, zg, 28)
                dve.memset(cc[:, 3:4], 0.0).then_inc(s("ada_done"), 8)
                dve.wait_ge(s("mod_ps"), 5)
                mod_cols(56, 72, bank(7)[:, 0:16])

                def ya(i, n):
                    for g in (2 * n, 2 * n + 1):
                        b, uses = cur.bank_use(g)
                        dve.wait_ge(halves_free, cur.half_of(n) + (HALVES + 1 + g % 2))
                        x = gt[:, 2 * g:2 * g + 2, :]
                        dve.tensor_tensor(x, x, bank(b).rearrange("p (k t) -> p k t", k=2), mul)\
                            .then_inc(bank_free[b], 1)
                walk(1, [0, 1], [0, 1], [0, 1, 0, 1], ya)
                link(dve.memset(att_exp, 0.0))
                for hh in range(HD // HG):
                    delta(hh)
                for c in range(2):
                    dve.wait_ge(s("yb_hi_ready"), c + 1)
                    sl = slice(4 * c, 4 * c + 4)
                    dve.tensor_tensor(u_lo[:, sl, :], qkv[:, sl, :], u_hi[:, sl, :].bitcast(F32), sub)\
                        .then_inc(s("yb_ready"), 1)

                def merge(i, n):
                    b, uses = cur.bank_use(n)
                    dve.wait_ge(halves_free, cur.half_of(n) + (HALVES + 2))
                    v = lambda x: x.rearrange("p (k t) -> p k t", k=2)
                    dve.tensor_tensor(mt, gt[:, KD + 2 * n:KD + 2 * n + 2, :], v(bank(b)), mul).then_inc(bank_free[b], 1)
                    dve.wait_ge(bank_free[b], uses + 1)
                    x = gt[:, 2 * n:2 * n + 2, :]
                    dve.tensor_tensor(x, x, mt, add).then_inc(s("mg_f"), 1)
                    dve.wait_ge(s("mg_hi_ready"), n + 1)
                    dve.tensor_tensor(mg_lo[:, 2 * n:2 * n + 2, :], x, mg_hi[:, 2 * n:2 * n + 2, :].bitcast(F32), sub)\
                        .then_inc(s("mg_ready"), 1)
                walk(1, [0, 1, 2, 3], range(4), [0, 1] * 2, merge)
                link(dve.tensor_copy(gcol[:, KD:2 * KD], modc[:, 40:48]))

                def close(i, n):
                    cur.done = cur.half_of(n) + (HALVES + 2)
                    residual(n, 2 * n, KD)
                walk(1, [0, 1, 2, 3], range(4), [0, 1] * 2, close)

            def delta(hh):
                hs = slice(hh * HG, hh * HG + HG)

                def t4(r):
                    return tk(r).rearrange("q (n h) -> q n h", n=4)[:, :, hs]

                def wide(x, w):
                    return x[:, :, None].broadcast_to([P, HG, w])

                def over(x, m):
                    return x[:, None, :].broadcast_to([P, m, CH])

                def halves(dst, src, n, last):
                    for side, rows in enumerate(SIDES):
                        for k in range(n.start, n.stop):
                            op = dve.tensor_copy(dst[rows, k, :, side * CH:(side + 1) * CH], src[rows, k, :, :])
                    op.then_inc(s(last), 1)
                ss = tk(TX, 16)
                for idx, (x, p) in enumerate(((ktm, 0), (ktm, 1), (qtm, 0), (qtm, 1))):
                    follow.next("d_ad")
                    w = tmpc[:, 0:2].rearrange("q n h c -> q (n h c)").rearrange("q (h c) -> q h c", h=HG)
                    link(dve.tensor_tensor(w, x[:, p], x[:, p], mul))
                    op = dve.tensor_reduce(ss[:, 4 * idx:4 * idx + 4], w, AX.X, add)
                    if idx < 3:
                        link(op)
                op.then_inc(s("d_da"), 1)
                follow.next("d_ad")
                follow.next("d_ad")
                rs = tk(TE, 16)
                link(dve.reciprocal(rs, rs))
                link(dve.tensor_scalar(rs[:, 8:16], rs[:, 8:16], float(P) ** -0.5, None, mul))
                for idx, (x, p) in enumerate(((ktm, 0), (ktm, 1), (qtm, 0), (qtm, 1))):
                    dve.tensor_tensor(x[:, p], x[:, p], wide(rs[:, 4 * idx:4 * idx + 4], P), mul).then_inc(s("d_dp"), 1)
                for n in range(4):
                    op = dve.tensor_tensor(tmpc[:, n], wide(t4(TGN)[:, n], CH), over(cs("c01" if n < 2 else "c23"), HG), mul)
                op.then_inc(s("d_dp"), 1)
                follow.next("d_pd")
                for n in range(4):
                    src = bank(2 + n // 2)[:, (n % 2) * S:(n % 2 + 1) * S].rearrange("q (h c) -> q h c", h=HG)
                    op = dve.tensor_tensor(dec[:, n], src, wide(t4(TGS)[:, n], CH), sub)
                link(op)
                for n in range(4):
                    op = dve.tensor_tensor(dec[:, n], dec[:, n], over(cs("neg01" if n < 2 else "neg23"), HG), add)
                op.then_inc(s("d_da"), 1)
                for n in range(4):
                    op = dve.tensor_tensor(tmpc[:, n], wide(t4(TBN)[:, n], CH), over(cs("identc"), HG), mul)
                op.then_inc(s("d_dp"), 1)
                follow.next("d_ad")
                follow.next("d_ad")
                for n in range(4):
                    p = PAIR[n]
                    for side, rows in enumerate(SIDES):
                        dve.tensor_tensor(att_exp[rows, n, :, side * CH:(side + 1) * CH], kk[rows, 1, p], dec[rows, n], mul)
                    op = dve.tensor_tensor(bmat[:, n], kk[:, 0, p], dec[:, n], mul)
                link(op)
                flat = lambda x: x.rearrange("q n h c -> q (n h) c")
                link(dve.tensor_tensor(flat(bmat), flat(bmat), over(cs("strict"), 4 * HG), mul))
                follow.next("d_pd")
                for j in range(2):
                    x = bmat[:, 2 * j:2 * j + 2].rearrange("q n h c -> q (n h c)")
                    op = dve.tensor_tensor(x, x, bank(4 + j), mul)
                link(op)
                link(dve.memset(r_exp, 0.0))
                halves(r_exp, bmat, slice(0, 4), "d_dp")
                lv = cs("levels").rearrange("q (l c) -> q l c", l=6)
                link(dve.tensor_tensor(flat(tmpc), flat(bmat), over(lv[:, 0], 4 * HG), mul))
                link(dve.tensor_tensor(flat(bmat), over(cs("identc"), 4 * HG), flat(tmpc), sub))
                follow.next("d_ad")
                halves(r_exp, bmat, slice(0, 4), "d_dp")
                with follow.loop(5, chain, 4, d_pd=2) as i:
                    for j in range(2):
                        n = slice(2 * j, 2 * j + 2)
                        follow.next("d_pd")
                        mask = lv[:, bass.ds(i + 1, 1), :].broadcast_to([P, 2 * HG, CH])
                        link(dve.tensor_tensor(flat(tmpc[:, n]), bank(2 + j).rearrange("q (m c) -> q m c", c=CH), mask, mul))
                        link(dve.tensor_tensor(bmat[:, n], bmat[:, n], tmpc[:, n], sub))
                        halves(r_exp, bmat, n, "d_dp")
                for n in range(4):
                    p = PAIR[n]
                    if n == 0:
                        dve.tensor_tensor(rr, vtm[:, p], wide(t4(TBN)[:, n], P), mul).then_inc(s("d_dp"), 1)
                    else:
                        dve.tensor_tensor(t1, vtm[:, p], wide(t4(TBN)[:, n], P), mul)
                        follow.next("d_pd")
                        link(dve.tensor_tensor(t2, bank(2).rearrange("q (h c) -> q h c", h=HG), wide(t4(TAB)[:, n], P), mul))
                        dve.tensor_tensor(rr, t1, t2, sub).then_inc(s("d_dp"), 1)
                        follow.next("d_pd")
                    follow.next("d_pd")
                    b4 = bank(4).rearrange("q (h c) -> q h c", h=HG)
                    dve.tensor_tensor(vns, b4, wide(t4(TED)[:, n], P), mul).then_inc(s("d_dp"), 1)
                    dve.tensor_copy(vn, b4).then_inc(s("d_dp"), 1)
                    if n < 3:
                        if n:
                            for d in range(2):
                                es = tok[:, TES + side_of(n, d), :].rearrange("q (n h) -> q n h", n=4)[:, n, hs]
                                op = dve.tensor_tensor(st[:, d], st[:, d], wide(es, P), mul)
                            link(op)
                        follow.next("d_pd")
                        for d in range(2):
                            bd = bank(6 + d).rearrange("q (h c) -> q h c", h=HG)
                            op = (dve.tensor_tensor(st[:, d], st[:, d], bd, add) if n else dve.tensor_copy(st[:, d], bd))
                        op.then_inc(s("d_dp"), 1)
                    if n:
                        link(dve.tensor_tensor(t3, bank(3).rearrange("q (h c) -> q h c", h=HG), wide(t4(TEG)[:, n], P), mul))
                        if n >= 2:
                            link(dve.tensor_tensor(t3, t3, oacc[:, p], add))
                    follow.next("d_pd")
                    b5 = bank(5).rearrange("q (h c) -> q h c", h=HG)
                    op = dve.tensor_tensor(oacc[:, p], t3, b5, add) if n else dve.tensor_copy(oacc[:, p], b5)
                    if n < 3:
                        op.then_inc(s("d_dp"), 1)
                    else:
                        link(op)
                link(dve.tensor_tensor(osq, oacc, oacc, mul))
                dve.tensor_reduce(tk(TX, 8), osq.rearrange("q p h c -> q (p h) c"), AX.X, add).then_inc(s("d_da"), 1)
                follow.next("d_ad")
                link(dve.reciprocal(tk(TE, 8), tk(TE, 8)))
                o8 = oacc.rearrange("q p h c -> q (p h) c")
                dve.tensor_tensor(o8, o8, tk(TE, 8)[:, :, None].broadcast_to([P, 8, P]), mul).then_inc(s("d_dp"), 1)
                for p in range(2):
                    follow.next("d_pd")
                    for h in range(HG):
                        t = hh * HG + h
                        op = dve.scalar_tensor_tensor(pair(qkv[:, t, :], p),
                                                      bank(2 + p)[:, h * P:(h + 1) * P].rearrange("q (c t) -> q c t", c=2),
                                                      prm[:, DN_NORM:DN_NORM + 1], pair(zs[:, t, :], p), mul, mul)
                op.then_inc(s("d_dp"), 1)
                if hh == 1:
                    dve.memset(cc[:, 3:4], 0.0).then_inc(s("d_da"), 2)

            def columns(iters, n, hook, last=False, links=0):
                walk(iters, SIX if n == 6 else list(range(4)), range(n), [0, 1] * (n // 2), hook, links)

            idle = lambda i, n: None

            def two(b):
                return bank(b).rearrange("p (k t) -> p k t", k=2)

            def add_h(g, n, t):
                b, uses = cur.bank_use(g)
                dve.wait_ge(halves_free, cur.half_of(n) + (HALVES + 2))
                x = hT[:, bass.ds(t, 2), :]
                dve.tensor_tensor(x, x, two(b), add).then_inc(bank_free[b], 1)

            def mlp(layer):
                norm(NRM["mlp"] + 8 * layer)

                def up(i, n):
                    b, uses = cur.bank_use(n)
                    r = (sil, sil2)[n % 2]
                    m = (mt, mt2)[n % 2]
                    dve.wait_ge(bank_free[b], uses + 1)
                    link(dve.tensor_tensor(m, r, r, mul))
                    dve.wait_ge(s("mid_hi_ready"), i * 4 + (22 + 16 * layer + n + 1))
                    t = bass.ds(i * 8 + 2 * n, 2)
                    dve.tensor_tensor(mid_lo[:, t, :], m, mid_hi[:, t, :].bitcast(F32), sub).then_inc(s("mid_ready"), 1)
                columns(4, 4, up, links=4)

                def down(o):
                    def hook(i, n):
                        if n % 4 == 3:
                            add_h(n // 4, n, i * 4 + (o + 2 * (n // 4)))
                    return hook
                if layer == 0:
                    walk(2, [0, 1, 2, 3] * 2, range(8), [0, 1], down(0))
                else:
                    walk(1, [0, 1, 2, 3] * 2, range(8), [0, 1], down(0))
                    walk(1, [0, 1, 2, 3] * 2, range(8), [0, 1], down(4), last=True)

            def attention():
                link(dve.tensor_tensor(lamv[:, 0:2, :], lamv[:, 0:2, :], lamv[:, 2:4, :], mul))
                dve.tensor_reduce(lam[:, 0:2], lamv[:, 0:2, :], AX.X, add).then_inc(s("a_lam"), 1)
                norm(NRM["attn"])
                dve.wait_ge(s("a_elam"), 1)
                link(dve.tensor_tensor(lam[:, 4:5], lam[:, 3:4], lam[:, 2:3], sub))
                link(dve.tensor_scalar(lam[:, 4:5], lam[:, 4:5], -LAMBDA_INIT, None, add))
                link(dve.tensor_scalar(lam[:, 6:7], prm[:, SUBLN:SUBLN + 1], 1.0 - LAMBDA_INIT, None, mul))
                dve.wait_ge(s("tz_in"), 16)
                dve.wait_ge(s("consts2_in"), 16)
                link(dve.tensor_tensor(tz[:, :, 0:S], tz[:, :, 0:S], cs2("causal")[:, None, :].broadcast_to([P, 8, S]), add))
                link(dve.tensor_copy(tz[:, :, S:S + P], tz[:, :, P:S]))
                columns(2, 6, idle)

                def scores(h):
                    dve.wait_ge(s("a_sc"), h + 1)
                    x = sc2[h % 2]
                    for m in range(2):
                        op = dve.scalar_tensor_tensor(x[:, m, :], bank(2 + 2 * (h % 2) + m)[:, 0:384], 64 ** -0.5,
                                                      tz[:, h, :], mul, add)
                    op.then_inc(s("a_sread"), 1)
                    dve.wait_ge(s("a_sread"), h + 1)
                    c = stat[:, 4 * (h % 2):4 * (h % 2) + 4].rearrange("p (m b) -> p m b", m=2)
                    dve.tensor_reduce(c[:, :, 0:1], x[:, :, 256:384], AX.X, ALU.max, negate=True)
                    dve.tensor_reduce(c[:, :, 1:2], x[:, :, 0:256], AX.X, ALU.max, negate=True).then_inc(s("a_max"), 1)

                scores(0)
                for h in range(8):
                    if h < 7:
                        scores(h + 1)
                    dve.wait_ge(s("a_exp"), h + 1)
                    x, a = sc2[h % 2], aa[h % 2]
                    r = stat[:, 8 + 4 * (h % 2):12 + 4 * (h % 2)]
                    link(dve.reciprocal(r, r))
                    link(dve.tensor_scalar(r[:, 2:4], r[:, 2:4], lam[:, 4:5], None, mul))
                    if h >= 2:
                        dve.wait_ge(s("a_T"), h - 1)
                    for blk, (o, n) in enumerate(((256, 128), (0, 256))):
                        op = dve.tensor_scalar(a1t[:, o:o + n], x[:, 1, o:o + n], r[:, 2 + blk:3 + blk], None, mul)
                    link(op)
                    for blk, (o, n) in enumerate(((256, 128), (0, 256))):
                        op = dve.scalar_tensor_tensor(a[:, o:o + n], x[:, 0, o:o + n], r[:, blk:blk + 1], a1t[:, o:o + n], mul, add)
                    op.then_inc(s("a_comb"), 1)
                dve.wait_ge(s("a_comb"), 8)
                dve.wait_ge(s("a_o"), 8)
                link(dve.tensor_tensor(osq2, otm, otm, mul))
                r = stat[:, 16:32]
                o16 = otm.rearrange("p t h c -> p (t h) c")
                dve.tensor_reduce(r, osq2.rearrange("p t h c -> p (t h) c"), AX.X, add).then_inc(s("a_ss"), 1)
                dve.wait_ge(s("a_rms"), 1)
                link(dve.reciprocal(r, r))
                dve.tensor_tensor(o16, o16, r[:, :, None].broadcast_to([P, 16, P]), mul).then_inc(s("a_on"), 1)
                for b in range(4):
                    dve.wait_ge(s("a_uhi"), b + 1)
                    sl = slice(2 * b, 2 * b + 2)
                    dve.tensor_tensor(u_lo[:, sl, :], uf[:, sl, :], u_hi[:, sl, :].bitcast(F32), sub).then_inc(s("a_ready"), 1)
                columns(1, 4, lambda i, n: add_h(n, n, 2 * n))

            def mlstm():
                for b in pad2:
                    op = dve.memset(b[:, :, 0:3], 0.0)
                op.then_inc(s("m_pads"), 1)
                norm(NRM["mlstm"])
                IG, X, T, LF, AR, CM, NCM, EM, ONE = range(9)
                row = lambda k: rows2[0:4, k, :]
                dve.wait_ge(s("m_gates"), 1)
                dve.tensor_scalar(row(IG), bank(3)[0:4, 0:S], bif[:, 0:1], None, add)
                link(dve.tensor_scalar(row(X), bank(3)[0:4, S:2 * S], bif[:, 1:2], None, add))
                dve.memset(row(ONE), 1.0)
                dve.scalar_tensor_tensor(row(T), row(X), -1.0, row(X), mul, ALU.max).then_inc(s("m_x"), 1)
                dve.wait_ge(s("m_ln"), 1)
                link(dve.scalar_tensor_tensor(row(LF), row(X), 0.0, row(T), ALU.min, sub))
                link(dve.tensor_tensor_scan(row(X), row(ONE), row(LF), 0.0, mul, add))
                link(dve.tensor_tensor(row(AR), row(IG), row(X), sub))
                link(dve.tensor_tensor_scan(row(CM), row(ONE), row(AR), 0.0, mul, ALU.max))
                link(dve.tensor_scalar(row(NCM), row(CM), -1.0, None, mul))
                dve.tensor_tensor(row(EM), row(X), row(CM), add).then_inc(s("m_m"), 1)

                def conv(i, n):
                    b, uses = cur.bank_use(n)
                    dve.wait_ge(bank_free[b], uses + 1)
                    if n >= 2:
                        dve.wait_ge(s("m_qk"), n - 1)
                    for t in range(4):
                        for m in range(2):
                            c = CONV2 + 8 * t + 2 * n + m
                            w, x, y = prm[:, c:c + 1], pad2[n % 2][:, m, t:t + S], cac2[n % 2][:, m, :]
                            op = (dve.tensor_scalar(y, x, w, None, mul) if t == 0 else
                                  dve.scalar_tensor_tensor(y, x, w, y, mul, add))
                        if t < 3:
                            link(op)
                    op.then_inc(s("m_conv"), 1)
                columns(1, 4, conv)
                columns(2, 4, idle)
                dve.wait_ge(s("m_o"), 1)

                def weights(h):
                    dve.wait_ge(s("m_s"), h + 1)
                    if h:
                        dve.wait_ge(s("m_num"), h)
                    dve.tensor_tensor(ex2[:, 0:S], bank(2)[:, 0:S], cs2("after"), add)
                    dve.tensor_tensor(ex2[:, S:S + P], bank(2)[:, P:S], cs2("after")[:, 0:P], add).then_inc(s("m_d"), 1)
                    dve.wait_ge(s("m_e"), h + 1)
                    dve.scalar_tensor_tensor(sct, bank(3)[:, 0:384], float(P) ** -0.5, ex2, mul, mul).then_inc(s("m_sc"), 1)

                for h in range(ML_H):
                    weights(h)
                    dve.wait_ge(s("m_den"), h + 1)
                    link(dve.tensor_tensor(dn, dn, bank(2)[:, S:2 * S], ALU.max))
                    dve.scalar_tensor_tensor(d2, dn, EPS, dn, mul, mul).then_inc(s("m_bcread"), 1)
                    dve.wait_ge(s("m_bcread"), h + 1)
                    dve.wait_ge(s("m_ss"), h + 1)
                    dve.scalar_tensor_tensor(rt, bank(6)[:, 0:S], 1.0 / 256, d2, mul, add).then_inc(s("m_r2"), 1)
                    dve.wait_ge(s("m_rms"), h + 1)
                    link(dve.reciprocal(rt, rt))
                    dve.tensor_tensor(yh, two(4), rt[:, None, :].broadcast_to([P, 2, S]), mul).then_inc(s("m_y"), 1)
                    dve.wait_ge(s("m_y"), h + 1)
                    for m in range(2):
                        k = 2 * h + m
                        op = dve.scalar_tensor_tensor(uf[:, k, :], yh[:, m, :], prm[:, HEAD_NORM + k:HEAD_NORM + k + 1],
                                                      vo[:, 8 + k, :], mul, mul)
                    op.then_inc(s("m_uf"), 1)
                    dve.wait_ge(s("m_uhi"), h + 1)
                    sl = slice(2 * h, 2 * h + 2)
                    dve.tensor_tensor(u_lo[:, sl, :], uf[:, sl, :], u_hi[:, sl, :].bitcast(F32), sub).then_inc(s("m_ready"), 1)
                columns(1, 4, lambda i, n: add_h(n, n, 2 * n))

            ffn(True, NRM["ffn1"], 0, 16, 0)
            mixer()
            ffn(False, NRM["ffn2"], 48, 64, 11)
            norm(NRM["final"], final=True, dst=hT)
            attention()
            mlp(0)
            mlstm()
            mlp(1)
            norm(NRM["final2"], final=True)


_INS = ["x", "c", "w_ada", "b_ada", "norm_ffn1", "w_ffn1_up", "w_ffn1_down", "norm_mix", "w_in", "conv_a", "conv_dn",
        "a_log_fwd", "dt_bias_fwd", "a_log_bwd", "dt_bias_bwd", "dn_norm", "w_a_out", "w_b_out", "w_out", "norm_ffn2",
        "w_ffn2_up", "w_ffn2_down", "norm_final", "rel_bias_2", "attn_norm_2", "attn_w_in_2", "attn_lambda_q1_2",
        "attn_lambda_k1_2", "attn_lambda_q2_2", "attn_lambda_k2_2", "attn_subln_2", "attn_w_out_2",
        "mlstm_norm_2", "mlstm_w_in_2", "mlstm_b_i_2", "mlstm_b_f_2", "mlstm_conv_w_2", "mlstm_conv_b_2",
        "mlstm_head_norm_2", "mlstm_w_out_2", "mlp_norm_2", "mlp_w1_2", "mlp_w2_2", "final_norm_2"]


def kernel(**inputs):
    import concourse.bacc as _bacc
    from concourse.bass_utils import run_bass_kernel_spmd as _run

    nc = _bacc.Bacc("TRN2", target_bir_lowering=False, num_devices=1)
    arrays, A = {}, {}
    for name in _INS:
        arrays["in_" + name] = np.ascontiguousarray(inputs[name])
    arrays["in_consts"], arrays["in_consts2"] = constants()[0], constants2()[0]
    for name, a in arrays.items():
        A[name[3:]] = nc.dram_tensor(name, a.shape, mybir.dt.from_np(a.dtype), kind="ExternalInput").ap()
    out = nc.dram_tensor("y", (1, S, D), F32, kind="ExternalOutput").ap()
    build(nc, A, out)
    return _run(nc, [arrays], core_ids=[0]).results[0]["y"]
```
